# Optimizing a Trainium2 kernel written in Bass

```python
import jax, jax.numpy as jnp
from jax import lax
import numpy as np

D_MODEL = 1024
BATCH = 1
SEQ = 128
DEPTH = 2
DEC_BATCH = 1
DEC_SEQ = 512
PAST_LEN = 128

GRID_W = 64
RET_HEADS = 4
RET_DK = 128
RET_DV = 256
RET_QK_W = RET_HEADS * RET_DK
RET_V_W = RET_HEADS * RET_DV
RET_CHUNK = 128
NA_HEADS = 8
NA_DH = 64
NA_W = NA_HEADS * NA_DH
NA_WIN_H = 8
NA_WIN_W = 16
Q_BLOCK = 128
D_FF = -(-8 * D_MODEL // (3 * 256)) * 256
ROPE_BASE = 10000.0
EPS = 1e-6
IN_WIDTHS = (RET_QK_W, RET_QK_W, RET_V_W, RET_V_W, NA_W, NA_W, NA_W)
IN_WIDTH = sum(IN_WIDTHS)

kernel_name = 'hybrid_retention_natten_diffusion_step'

def rmsnorm(x, g):
    xf = x.astype(jnp.float32)
    y = xf * lax.rsqrt(jnp.mean(xf * xf, axis=-1, keepdims=True) + EPS)
    return (y * g.astype(jnp.float32)).astype(x.dtype)

def adaln(cvec, w_ada, b_ada):
    return jnp.split(jax.nn.silu(cvec) @ w_ada + b_ada, 6, axis=-1)

def modulate(h, shift, scale):
    return h * (1 + scale[:, None, :]) + shift[:, None, :]

def project_in(hm, w_in):
    b, l = hm.shape[:2]
    points = [int(p) for p in np.cumsum(IN_WIDTHS)[:-1]]
    rq, rk, rv, rg, nq, nk, nv = jnp.split(hm @ w_in, points, axis=-1)
    return (rq.reshape(b, l, RET_HEADS, RET_DK), rk.reshape(b, l, RET_HEADS, RET_DK),
            rv.reshape(b, l, RET_HEADS, RET_DV), rg,
            nq.reshape(b, l, NA_HEADS, NA_DH), nk.reshape(b, l, NA_HEADS, NA_DH),
            nv.reshape(b, l, NA_HEADS, NA_DH))

def rope_2d(x):
    l = x.shape[1]
    t = jnp.arange(l)
    row = (t // GRID_W).astype(jnp.float32)
    col = (t % GRID_W).astype(jnp.float32)
    n_freq = x.shape[-1] // 4
    inv = ROPE_BASE ** (-jnp.arange(n_freq, dtype=jnp.float32) / n_freq)
    ang = jnp.concatenate([row[:, None] * inv, col[:, None] * inv], axis=-1)
    cos = jnp.cos(ang)[None, :, None, :]
    sin = jnp.sin(ang)[None, :, None, :]
    x1, x2 = jnp.split(x.astype(jnp.float32), 2, axis=-1)
    return jnp.concatenate([x1 * cos - x2 * sin, x1 * sin + x2 * cos], axis=-1).astype(x.dtype)

def retention_chunked(q, k, v, log_gamma, s0):
    b, l, h, dk = q.shape
    dv = v.shape[-1]
    n = l // RET_CHUNK
    pos = jnp.arange(RET_CHUNK, dtype=jnp.float32)
    rel = pos[:, None] - pos[None, :]
    decay_in = jnp.where(rel >= 0, jnp.exp(log_gamma[:, None, None] * jnp.maximum(rel, 0.0)), 0.0)
    xi = jnp.exp(log_gamma[:, None] * (pos + 1.0)).T[None, :, :, None]
    zeta = jnp.exp(log_gamma[:, None] * (RET_CHUNK - 1.0 - pos)).T[None, :, :, None]
    g_chunk = jnp.exp(log_gamma * RET_CHUNK)[None, :, None, None]

    def chunks(a):
        return jnp.moveaxis(a.reshape(b, n, RET_CHUNK, *a.shape[2:]), 1, 0)

    def step(s, inp):
        qc, kc, vc = inp
        scores = jnp.einsum('bnhd,bmhd->bhnm', qc, kc) * decay_in
        inner = jnp.einsum('bhnm,bmhe->bnhe', scores, vc)
        cross = jnp.einsum('bnhd,bhde->bnhe', qc, s) * xi
        s_new = g_chunk * s + jnp.einsum('bmhd,bmhe->bhde', kc * zeta, vc)
        return s_new, inner + cross

    s_fin, out = lax.scan(step, s0, (chunks(q), chunks(k), chunks(v)))
    return jnp.moveaxis(out, 0, 1).reshape(b, l, h, dv), s_fin

def retention_bidir(q, k, v, log_g, s0_f, s0_b):
    y_f, s_f = retention_chunked(q, k, v, log_g[0], s0_f)
    fl = lambda a: jnp.flip(a, axis=1)
    y_b, s_b = retention_chunked(fl(q), fl(k), fl(v), log_g[1], s0_b)
    return y_f + fl(y_b), s_f, s_b

def retention_output(y, gate, gn_gain):
    b, l = y.shape[:2]
    mu = jnp.mean(y, axis=-1, keepdims=True)
    var = jnp.mean(jnp.square(y - mu), axis=-1, keepdims=True)
    yn = ((y - mu) * lax.rsqrt(var + EPS)).reshape(b, l, RET_V_W) * gn_gain.astype(jnp.float32)
    return (jax.nn.silu(gate.astype(jnp.float32)) * yn).astype(gate.dtype)

def context_attention(q, k, v):
    b, lc, h, d = q.shape
    nb = lc // Q_BLOCK
    qb = jnp.moveaxis(q.reshape(b, nb, Q_BLOCK, h, d), 1, 0)

    def blk(qi):
        s = jnp.einsum('bqhd,bkhd->bhqk', qi, k).astype(jnp.float32)
        p = jax.nn.softmax(s, axis=-1).astype(v.dtype)
        return jnp.einsum('bhqk,bkhd->bqhd', p, v)

    o = lax.map(blk, qb)
    return jnp.moveaxis(o, 0, 1).reshape(b, lc, h * d)

def neighbourhood_attention(q, k, v, k_ctx, v_ctx, rpb):
    b, l, h, d = q.shape
    rows = l // GRID_W
    wh = min(NA_WIN_H, rows)
    ww = NA_WIN_W
    n_keys = wh * ww
    cols = jnp.arange(GRID_W)
    col_start = jnp.clip(cols - ww // 2, 0, GRID_W - ww)
    key_cols = col_start[:, None] + jnp.arange(ww)[None, :]
    col_off = key_cols - cols[:, None] + (NA_WIN_W - 1)
    q_rows = jnp.moveaxis(q.reshape(b, rows, GRID_W, h, d), 1, 0)

    def row_block(args):
        r, qr = args
        row_start = jnp.clip(r - wh // 2, 0, rows - wh)
        key_rows = row_start + jnp.arange(wh)
        idx = (key_rows[None, :, None] * GRID_W + key_cols[:, None, :]).reshape(GRID_W * n_keys)
        kw = jnp.take(k, idx, axis=1).reshape(b, GRID_W, n_keys, h, d)
        vw = jnp.take(v, idx, axis=1).reshape(b, GRID_W, n_keys, h, d)
        row_off = key_rows - r + (NA_WIN_H - 1)
        bias = rpb[:, row_off[:, None, None], col_off[None, :, :]]
        bias = jnp.transpose(bias, (0, 2, 1, 3)).reshape(h, GRID_W, n_keys).astype(jnp.float32)
        s_loc = jnp.einsum('bwhd,bwkhd->bhwk', qr, kw).astype(jnp.float32) + bias
        s_ctx = jnp.einsum('bwhd,bshd->bhws', qr, k_ctx).astype(jnp.float32)
        p = jax.nn.softmax(jnp.concatenate([s_loc, s_ctx], axis=-1), axis=-1).astype(v.dtype)
        return (jnp.einsum('bhwk,bwkhd->bwhd', p[..., :n_keys], vw)
                + jnp.einsum('bhws,bshd->bwhd', p[..., n_keys:], v_ctx))

    o = lax.map(row_block, (jnp.arange(rows), q_rows))
    return jnp.moveaxis(o, 0, 1).reshape(b, l, h * d)

def swiglu(h, wg, wu, wd):
    return (jax.nn.silu(h @ wg) * (h @ wu)) @ wd

def block_tail(x, hm, y_ret, y_na, g1, sh2, sc2, g2, w_ret_out, w_na_out, w_gate, w_o,
               n_post_mix, n_pre_ffn, n_post_ffn, w_ffn_gate, w_ffn_up, w_ffn_down):
    g_ret, g_na = jnp.split(jax.nn.sigmoid(hm @ w_gate), 2, axis=-1)
    mixed = (g_ret * (y_ret @ w_ret_out) + g_na * (y_na @ w_na_out)) @ w_o
    x = x + g1[:, None, :] * rmsnorm(mixed, n_post_mix)
    hf = modulate(rmsnorm(x, n_pre_ffn), sh2, sc2)
    return x + g2[:, None, :] * rmsnorm(swiglu(hf, w_ffn_gate, w_ffn_up, w_ffn_down), n_post_ffn)

def setup_inputs(seed: int = 0) -> dict:
    key = jax.random.key(seed)
    ks = jax.random.split(key, 24)
    f32 = jnp.float32
    nrm = lambda k, shape, s: jax.random.normal(k, shape, f32) * s
    gamma0 = 1.0 - 2.0 ** (-5.0 - np.arange(RET_HEADS, dtype=np.float32))
    logit0 = jnp.asarray(np.log(gamma0 / (1.0 - gamma0)), f32)
    return {
        'x_prompt': nrm(ks[0], (BATCH, SEQ, D_MODEL), 1.0),
        'x_sample': nrm(ks[1], (DEC_BATCH, DEC_SEQ, D_MODEL), 1.0),
        'cache_na_k': nrm(ks[2], (DEC_BATCH, DEPTH, PAST_LEN, NA_HEADS, NA_DH), 1.0),
        'cache_na_v': nrm(ks[3], (DEC_BATCH, DEPTH, PAST_LEN, NA_HEADS, NA_DH), 1.0),
        'state_ret': nrm(ks[4], (DEC_BATCH, DEPTH, 2, RET_HEADS, RET_DK, RET_DV), 0.5),
        'c': nrm(ks[5], (DEC_BATCH, D_MODEL), 1.0),
        'c_ctx': nrm(ks[6], (D_MODEL,), 1.0),
        'w_ada': nrm(ks[7], (DEPTH, D_MODEL, 6 * D_MODEL), 0.5 * D_MODEL ** -0.5),
        'b_ada': nrm(ks[8], (DEPTH, 6 * D_MODEL), 0.01),
        'norm_pre_mix': 1.0 + nrm(ks[9], (DEPTH, D_MODEL), 0.05),
        'norm_post_mix': 1.0 + nrm(ks[10], (DEPTH, D_MODEL), 0.05),
        'norm_pre_ffn': 1.0 + nrm(ks[11], (DEPTH, D_MODEL), 0.05),
        'norm_post_ffn': 1.0 + nrm(ks[12], (DEPTH, D_MODEL), 0.05),
        'w_in': nrm(ks[13], (DEPTH, D_MODEL, IN_WIDTH), D_MODEL ** -0.5),
        'ret_decay_logit': logit0[None, None, :] + nrm(ks[14], (DEPTH, 2, RET_HEADS), 0.1),
        'ret_gn_gain': 1.0 + nrm(ks[15], (DEPTH, RET_V_W), 0.05),
        'na_rpb': nrm(ks[16], (DEPTH, NA_HEADS, 2 * NA_WIN_H - 1, 2 * NA_WIN_W - 1), 0.02),
        'w_ret_out': nrm(ks[17], (DEPTH, RET_V_W, D_MODEL), RET_V_W ** -0.5),
        'w_na_out': nrm(ks[18], (DEPTH, NA_W, D_MODEL), NA_W ** -0.5),
        'w_gate': nrm(ks[19], (DEPTH, D_MODEL, 2 * D_MODEL), D_MODEL ** -0.5),
        'w_o': nrm(ks[20], (DEPTH, D_MODEL, D_MODEL), D_MODEL ** -0.5),
        'w_ffn_gate': nrm(ks[21], (DEPTH, D_MODEL, D_FF), D_MODEL ** -0.5),
        'w_ffn_up': nrm(ks[22], (DEPTH, D_MODEL, D_FF), D_MODEL ** -0.5),
        'w_ffn_down': nrm(ks[23], (DEPTH, D_FF, D_MODEL), D_FF ** -0.5),
    }

def reference(x_prompt, x_sample, cache_na_k, cache_na_v, state_ret, c, c_ctx, w_ada, b_ada,
              norm_pre_mix, norm_post_mix, norm_pre_ffn, norm_post_ffn, w_in, ret_decay_logit,
              ret_gn_gain, na_rpb, w_ret_out, w_na_out, w_gate, w_o, w_ffn_gate, w_ffn_up,
              w_ffn_down):
    f32 = jnp.float32
    q_scale = NA_DH ** -0.5
    k_scale = RET_DK ** -0.5

    x = x_prompt
    b_p = x.shape[0]
    k_list, v_list, s_list = [], [], []
    for l in range(DEPTH):
        sh1, sc1, g1, sh2, sc2, g2 = adaln(c_ctx[None, :], w_ada[l], b_ada[l])
        hm = modulate(rmsnorm(x, norm_pre_mix[l]), sh1, sc1)
        rq, rk, rv, rg, nq, nk, nv = project_in(hm, w_in[l])
        log_g = jax.nn.log_sigmoid(ret_decay_logit[l].astype(f32))
        s0 = jnp.zeros((b_p, RET_HEADS, RET_DK, RET_DV), f32)
        y, s_f, s_b = retention_bidir(rq.astype(f32), rk.astype(f32) * k_scale, rv.astype(f32),
                                      log_g, s0, s0)
        y_ret = retention_output(y, rg, ret_gn_gain[l])
        y_na = context_attention(nq * q_scale, nk, nv)
        x = block_tail(x, hm, y_ret, y_na, g1, sh2, sc2, g2, w_ret_out[l], w_na_out[l], w_gate[l],
                       w_o[l], norm_post_mix[l], norm_pre_ffn[l], norm_post_ffn[l],
                       w_ffn_gate[l], w_ffn_up[l], w_ffn_down[l])
        k_list.append(nk)
        v_list.append(nv)
        s_list.append(jnp.stack([s_f, s_b], axis=1).astype(x_prompt.dtype))
    y_prompt = x
    new_cache_na_k = jnp.stack(k_list, axis=1)
    new_cache_na_v = jnp.stack(v_list, axis=1)
    new_state_ret = jnp.stack(s_list, axis=1)

    x = x_sample
    for l in range(DEPTH):
        sh1, sc1, g1, sh2, sc2, g2 = adaln(c, w_ada[l], b_ada[l])
        hm = modulate(rmsnorm(x, norm_pre_mix[l]), sh1, sc1)
        rq, rk, rv, rg, nq, nk, nv = project_in(hm, w_in[l])
        rq = rope_2d(rq)
        rk = rope_2d(rk)
        log_g = jax.nn.log_sigmoid(ret_decay_logit[l].astype(f32))
        y, _, _ = retention_bidir(rq.astype(f32), rk.astype(f32) * k_scale, rv.astype(f32), log_g,
                                  state_ret[:, l, 0].astype(f32), state_ret[:, l, 1].astype(f32))
        y_ret = retention_output(y, rg, ret_gn_gain[l])
        y_na = neighbourhood_attention(nq * q_scale, nk, nv, cache_na_k[:, l], cache_na_v[:, l],
                                       na_rpb[l])
        x = block_tail(x, hm, y_ret, y_na, g1, sh2, sc2, g2, w_ret_out[l], w_na_out[l], w_gate[l],
                       w_o[l], norm_post_mix[l], norm_pre_ffn[l], norm_post_ffn[l],
                       w_ffn_gate[l], w_ffn_up[l], w_ffn_down[l])
    y_sample = x
    return (y_prompt, y_sample, new_cache_na_k, new_cache_na_v, new_state_ret)


_drawn_inputs = setup_inputs


def setup_inputs(seed=0):
    import zlib

    import numpy as np

    out = dict(_drawn_inputs(seed))
    spreads = {}
    factors = {'norm_post_ffn': 2.787, 'na_rpb': 45.981}
    for name, (base, spread) in spreads.items():
        noise = np.random.default_rng([zlib.crc32(name.encode()), seed]).standard_normal(out[name].shape)
        drawn = base * np.exp(spread * noise) if base else spread * noise
        out[name] = __import__('jax').numpy.asarray(drawn.astype(out[name].dtype))
    for name, factor in factors.items():
        out[name] = (out[name] * factor).astype(out[name].dtype)
    return out
```

```python
from contextlib import ExitStack, contextmanager

import numpy as np

import concourse.bass as bass
from concourse import mybir

P = 128
D = 1024
KD = D // P
NS, NP_ = 512, 128
T = NS + NP_
HALF = T // 2
DEPTH = 2
RH, DV = 4, 256
NPAIR = 4
GW, GR = 64, 8
WIN = 16
DFF = 2816
FB = DFF // 256
SLAB = 2048
ADA = 6 * D // 256
MAIN = 58
NPAR = 5 * KD + 6 * KD
EPS = 1e-6
OPEN = 1
K_SCALE = P ** -0.5
Q_SCALE = 64 ** -0.5
BIG = 1e30

F32 = mybir.dt.float32
F32R = mybir.dt.float32r
F16 = mybir.dt.float16
ACT = mybir.ActivationFunctionType
ALU = mybir.AluOpType

N_PRE_MIX, N_POST_MIX, N_PRE_FFN, N_POST_FFN, GN, B_ADA = (KD * i for i in range(6))
SH1, SC1, G1, SH2, SC2, G2 = (KD * i for i in range(6))

BLOCKS = [(0, 2, 0), (0, 3, 1), (1, 3, 1), (2, 2, 2)]
KIND_W = [256, 384, 256]
KIND_AT = [0, 384, 896]
STRIP_AT = [128, 0, 0]
MASK_AT = [0, 256, 640]
BIASW = 1280
DIAG, CTX_DIAG = 384, 896
RELW = 2 * NS


class Tally:

    def __init__(self, step=1):
        self.step, self.count, self.loops = step, 0, []

    def add(self, n=1):
        self.count += n * self.step

    def value(self, more=0):
        v = self.count + more * self.step
        for i, per in self.loops:
            v = i * per + v
        return v


class Units(Tally):

    def __init__(self, eng, tiles, ready, free):
        super().__init__()
        self.eng, self.tiles, self.ready, self.free = eng, tiles, ready, free

    def uses(self, back=0):
        v = (self.count - back) // 2
        for i, per in self.loops:
            assert per % 2 == 0
            v = i * (per // 2) + v
        return v

    def tile(self, back=0):
        return self.tiles[(self.count - back) % 2]

    def take(self):
        self.eng.wait_ge(self.free[self.count % 2], self.uses() + OPEN)
        return self.tile()

    def give(self, instruction):
        instruction.then_inc(self.ready, 1)
        self.add()

    def get(self):
        self.eng.wait_ge(self.ready, self.value(1))
        return self.tile()

    def release(self, instruction):
        instruction.then_inc(self.free[self.count % 2], 1)
        self.add()

    def wait_all_done(self):
        self.eng.wait_ge(self.ready, self.value())

    def wait_released(self, back):
        self.eng.wait_ge(self.free[(self.count - back) % 2], self.uses(back) + 1 + OPEN)


class Slabs(Tally):

    def slot(self):
        return self.count % 2

    def uses(self):
        v = self.count // 2
        for i, per in self.loops:
            assert per % 2 == 0
            v = i * (per // 2) + v
        return v


@contextmanager
def loop(eng, trips, tallies):
    before = {t: t.count for t in tallies}
    with eng.Fori(0, trips) as i:
        for t, per in tallies.items():
            t.loops.append((i, per * t.step))
        yield i
    for t, per in tallies.items():
        assert t.count - before[t] == per * t.step, (per, (t.count - before[t]) / t.step)
        t.loops.pop()
        t.count = before[t] + trips * per * t.step


def build(nc, x_in, w_main, w_down, w_ada, params, decay, state_in, ctx_k, ctx_v, strips, cvec,
          rope_in, rel_in, pos_in, mask_in, zpos_in, ident_in,
          x_out, k_out, v_out, state_out, x_keep):
    ctx = ExitStack()
    with ctx:
        arena0 = -(-nc.sbuf_base // 32) * 32
        room = nc.sbuf_usable_end - arena0
        nc.alloc_sbuf_tensor("arena", [P, (room - 64) // 4], F32)
        top = [0]

        def at(name, shape, offset, dt=F32):
            return nc.alloc_sbuf_tensor_at(name, shape, dt, offset=arena0 + offset)

        def fixed(name, shape, dt=F32):
            n = int(np.prod(shape[1:])) * (2 if dt in (F16,) else 4)
            t = at(name, shape, top[0], dt)
            top[0] += -(-n // 32) * 32
            return t

        def sem(name):
            return ctx.enter_context(nc.semaphore(name))

        hmh = fixed("hmh", [P, KD, T], F32R)
        hml = fixed("hml", [P, KD, T], F32R)
        raw = [fixed(f"raw{s}", [P, SLAB]) for s in range(2)]
        wh = [fixed(f"wh{s}", [P, SLAB], F32R) for s in range(2)]
        wl = [fixed(f"wl{s}", [P, SLAB], F32R) for s in range(2)]
        rope = fixed("rope", [P, 2, NS])
        rel = fixed("rel", [P, RELW], F16)
        pos = fixed("pos", [P, 2, NS], F16)
        mask = fixed("mask", [P, 896], F16)
        zpos = fixed("zpos", [P, 2])
        ident = fixed("ident", [P, P])
        ones = fixed("ones", [P, P])
        par_all = fixed("par_all", [P, DEPTH, NPAR])
        decay_all = fixed("decay_all", [P, DEPTH, 2 * RH])
        par = fixed("par", [P, NPAR])
        lg = fixed("lg", [P, 2 * RH])
        lt = fixed("lt", [P, 6, 2 * RH])
        lgh = fixed("lgh", [P, 3])
        gainh = fixed("gainh", [P, 2])
        zh = fixed("zh", [P, 2])
        cv = fixed("cv", [P, KD, 2])
        cs = fixed("cs", [P, KD, 2])
        mod = fixed("mod", [P, 6 * KD, 2])
        am1 = fixed("am1", [P, KD, 2])
        am2 = fixed("am2", [P, KD, 2])
        gm1 = fixed("gm1", [P, KD, 2])
        gm2 = fixed("gm2", [P, KD, 2])
        epsc = fixed("epsc", [P, 1])
        sums = fixed("sums", [P, 10])
        rsum = fixed("rsum", [P, 10])
        nmax = fixed("nmax", [P, 10])
        Z = top[0]

        class Map:
            def __init__(self, start):
                self.p = Z + start

            def __call__(self, name, shape, dt=F32):
                n = int(np.prod(shape[1:])) * (2 if dt in (F16,) else 4)
                t = at(name, shape, self.p, dt)
                self.p += -(-n // 32) * 32
                assert self.p <= room, (name, self.p, room)
                return t

        B = KD * T * 4
        merged = at("merged", [P, KD, T], Z)
        mix = at("mix", [P, KD, T], Z)
        x = at("x", [P, KD, T], Z + B)
        yret = at("yret", [P, KD, T], Z + B)
        r0 = Map(0)
        qs = r0("qs", [P, T]); ks = r0("ks", [P, T])
        kz_at = r0.p - Z
        qsw = r0("qsw", [P, NS]); ksw = r0("ksw", [P, NS])
        sg = r0("sg", [P, 2, T]); st = r0("st", [P, 2, DV]); xf = r0("xf", [P, 2, NS])
        assert r0.p <= Z + B, r0.p - Z - B
        r1 = Map(2 * B)
        qh = r1("qh", [P, T], F32R); ql = r1("ql", [P, T], F32R)
        kh = r1("kh", [P, T], F32R); kl = r1("kl", [P, T], F32R)
        qdh = r1("qdh", [P, 2, NS], F32R); qdl = r1("qdl", [P, 2, NS], F32R)
        vh = r1("vh", [P, 5, DV], F32R); vl = r1("vl", [P, 5, DV], F32R)
        ph = r1("ph", [P, 4 * NS + P], F32R); pl = r1("pl", [P, 4 * NS + P], F32R)
        dst = r1("dst", [P, RELW])
        s0r = r1("s0r", [P, 2, DV]); s0h = r1("s0h", [P, 2, DV], F32R); s0l = r1("s0l", [P, 2, DV], F32R)
        y = r1("y", [P, 2, T])
        pst_at = r1.p
        pst = r1("pst", [P, 2, NS])
        r1.p = pst_at
        sq2 = r1("sq2", [P, 2, T])
        r2 = Map(kz_at)
        kz = r2("kz", [P, 2, P]); kzh = r2("kzh", [P, 2, P], F32R); kzl = r2("kzl", [P, 2, P], F32R)
        a0 = Map(2 * B)
        ada = [a0(f"ada{s}", [P, KD, 256]) for s in range(4)]
        m0 = Map(2 * B)
        yrh = m0("yrh", [P, KD, T], F32R); yrl = m0("yrl", [P, KD, T], F32R)
        gate = m0("gate", [P, 2, T])
        n0 = Map(B)
        yna = n0("yna", [P, NPAIR, T])
        nva = n0.p
        nvh = n0("nvh", [P, 5, NS], F32R); nvl = n0("nvl", [P, 5, NS], F32R)
        nqh = n0("nqh", [P, T], F32R); nql = n0("nql", [P, T], F32R)
        nkh = n0("nkh", [P, T], F32R); nkl = n0("nkl", [P, T], F32R)
        ckr = n0("ckr", [P, P]); ckh = n0("ckh", [P, P], F32R); ckl = n0("ckl", [P, P], F32R)
        cvr = n0("cvr", [P, NS]); cvh = n0("cvh", [P, NS], F32R); cvl = n0("cvl", [P, NS], F32R)
        bias = n0("bias", [P, BIASW]); strip = n0("strip", [P, 2, 384])
        s = n0("s", [P, 2, NS])
        pth = n0("pth", [P, 2, NS], F32R); ptl = n0("ptl", [P, 2, NS], F32R)
        o = n0("o", [P, 5, P]); nkst = n0("nkst", [P, P]); nvst = n0("nvst", [P, NS])
        m1 = Map(B)
        m1.p = nva
        ynh = m1("ynh", [P, NPAIR, T], F32R); ynl = m1("ynl", [P, NPAIR, T], F32R)
        gate4 = m1("gate4", [P, 4, T]); mtmp = m1("mtmp", [P, T])
        m2 = Map(0); m2.p = m1.p
        mh = m2("mh", [P, KD, T], F32R); ml = m2("ml", [P, KD, T], F32R)
        f0 = Map(2 * B)
        hidh = f0("hidh", [P, 2, 2, T], F32R); hidl = f0("hidl", [P, 2, 2, T], F32R)
        draw = f0("draw", [P, 2, D])
        dwh = f0("dwh", [P, 2, D], F32R); dwl = f0("dwl", [P, 2, D], F32R)
        sig = f0("sig", [P, T]); hid = f0("hid", [P, T])
        scratch_b = [f0(f"{n}_b", [P, T]) for n in ("ssq", "rstd")] + [f0("sq_b", [P, 2, T])]
        f1 = Map(2 * B)
        scratch_a = [f1(f"{n}_a", [P, T]) for n in ("ssq", "rstd")] + [f1("sq_a", [P, 2, T]), f1("ff_a", [P, 2, T])]
        assert f1.p <= m1.p
        scratch_b.append(Map(2 * B)("ff_b", [P, 2, T]))

        unit = [ctx.enter_context(nc.psum_tensor(f"unit{i}", [P, 2, 512], F32)) for i in range(2)]
        sc = [ctx.enter_context(nc.psum_tensor(f"sc{i}", [P, 512], F32)) for i in range(2)]
        tp = [ctx.enter_context(nc.psum_tensor(f"tp{i}", [P, 512], F32)) for i in range(2)]

        def sems(names):
            return [sem(n) for n in names.split()]

        raw_in, w_hi, w_lo = ([sem(f"{n}{i}") for i in range(2)] for n in ("raw_in", "w_hi", "w_lo"))
        ada_in = [sem(f"ada_in{i}") for i in range(4)]
        unit_ready = sem("unit_ready")
        carried = sem("carried")
        unit_free = [sem(f"unit_free{i}") for i in range(2)]
        unit_hi, const_in, const_set, ada_used, cs_ready, mod_ready = sems("unit_hi const_in const_set ada_used cs_ready mod_ready")
        d_in, d_hi, d_lo = sems("d_in d_hi d_lo")
        sq_ready, sq_used, rstd_ready, xt_ready, f_ready, hm_ready = sems("sq_ready sq_used rstd_ready xt_ready f_ready hm_ready")
        osq_ready, ssq_added, accg_ready, xn_ready, x_saved, x_back = sems("osq_ready ssq_added accg_ready xn_ready x_saved x_back")
        lg_e, lg_z, lgh_ready, dexp_ready, swap_ready, roped, qk_hi, qk_ready = sems("lg_e lg_z lgh_ready dexp_ready swap_ready roped qk_hi qk_ready")
        qd_full, qd_hi, qd_ready, s0_in, s0_hi, s0_ready = sems("qd_full qd_hi qd_ready s0_in s0_hi s0_ready")
        sc_ready, p_full, p_hi, p_ready, kt_ready, kz_hi, kz_ready = sems("sc_ready p_full p_hi p_ready kt_ready kz_hi kz_ready")
        st_psum, st_ready, st_saved, ysq_ready, yret_ready = sems("st_psum st_ready st_saved ysq_ready yret_ready")
        yr_hi, yr_ready, merged_ready, yn_hi, yn_ready, m_hi, m_ready = sems("yr_hi yr_ready merged_ready yn_hi yn_ready m_hi m_ready")
        ck_in, ck_hi, ck_ready, cv_in, cv_hi, cv_ready, strip_in, strip_used = sems("ck_in ck_hi ck_ready cv_in cv_hi cv_ready strip_in strip_used")
        nsc_ready, s_ready, e_ready, t_ready, pt_hi, pt_ready, pt_used = sems("nsc_ready s_ready e_ready t_ready pt_hi pt_ready pt_used")
        nkst_ready, nvst_ready, nk_saved, nv_saved, y_saved = sems("nkst_ready nvst_ready nk_saved nv_saved y_saved")
        hid_hi, hid_ready = sems("hid_hi hid_ready")

        block = ctx.enter_context(nc.Block())

        def f32(ap):
            return ap.bitcast(F32)

        def wait_constants(engine):
            engine.wait_ge(const_in, 16 * 6)
            for s_ in (st_saved, nk_saved, nv_saved):
                engine.wait_ge(s_, 16)

        def carry(engine):
            engine.sem_inc(carried, 1)

        def halves(ap):
            return ap.rearrange("p (a b) -> p a b", a=2)

        def flat(ap):
            return ap.rearrange("p a b -> p (a b)")

        def row(ap):
            if len(ap.shape) == 3:
                return ap.rearrange("a p n -> (a p) n")
            return ap.rearrange("a p b n -> (a p) b n")

        STREAMS = ((0, slice(0, NS)), (1, slice(NS, T)))

        @block.sync
        def _(sp):
            split = Tally()
            with loop(sp, DEPTH * MAIN // 2 + 1, {split: 1}) as i:
                for n in range(2):
                    sp.wait_ge(w_lo[n], split.value() + OPEN)
                    sp.dma_start(raw[n][:, :], row(w_main[bass.ds(i * 2 + n, 1), :, :])).then_inc(raw_in[n], 16)
                split.add()

        @block.gpsimd
        def _(g):
            for s_ in (*unit_free, *w_lo, accg_ready, ada_used, s0_ready, ck_ready, strip_used, ssq_added,
                       d_lo):
                g.sem_inc(s_, OPEN)
            g.memset(ones[:, :], 1.0).then_inc(const_set, 1)
            g.memset(epsc[:, :], EPS).then_inc(const_set, 1)
            g.dma_start(x[:, :, :], x_in).then_inc(x_back, 16)
            for to, of in ((par_all[:, :, :], params), (ident[:, :], ident_in), (rope[:, :, :], rope_in),
                           (rel[:, :], rel_in), (pos[:, :, :], pos_in), (mask[:, :], mask_in)):
                g.dma_start(to, of).then_inc(const_in, 16)
            g.dma_start(cv[:, :, :], cvec).then_inc(st_saved, 16)
            g.dma_start(decay_all[:, :, :], decay).then_inc(nk_saved, 16)
            g.dma_start(zpos[:, :], zpos_in).then_inc(nv_saved, 16)
            lay, used, heads, pairs, downs = Tally(), Tally(), Tally(), Tally(), Tally()
            with loop(g, DEPTH, {lay: 1, used: ADA, heads: RH, pairs: NPAIR, downs: FB}) as l:
                g.wait_ge(accg_ready, lay.value() * KD + OPEN)
                carry(g)
                with loop(g, ADA // 4, {used: 4}) as i:
                    for n in range(4):
                        g.wait_ge(ada_used, used.value() + OPEN)
                        carry(g)
                        g.dma_start(ada[n][:, :, :],
                                    w_ada[bass.ds(l * ADA + i * 4 + n, 1), :, :].rearrange("a p (k n) -> (a p) k n", k=KD))\
                         .then_inc(ada_in[n], 16)
                    used.add(4)
                g.wait_ge(hm_ready, lay.value() * 2 * KD + KD)
                carry(g)
                g.dma_start(x_keep, x[:, :, :]).then_inc(x_saved, 16)
                with loop(g, RH, {heads: 1}) as h:
                    g.wait_ge(s0_ready, heads.value() + OPEN)
                    carry(g)
                    g.dma_start(s0r[:, :, :], row(state_in[bass.ds(l * RH + h, 1), :, :, :])).then_inc(s0_in, 16)
                    g.wait_ge(st_ready, heads.value(1))
                    carry(g)
                    g.dma_start(row(state_out[bass.ds(l * RH + h, 1), :, :, :]), st[:, :, :]).then_inc(st_saved, 16)
                    heads.add()
                g.wait_ge(merged_ready, lay.value() * 2 * KD + KD)
                carry(g)
                g.dma_start(cvr[:, :], row(ctx_v[bass.ds(l, 1), :, :])).then_inc(cv_in, 16)
                with loop(g, NPAIR, {pairs: 1}) as p:
                    g.wait_ge(ck_ready, pairs.value() + OPEN)
                    carry(g)
                    g.dma_start(ckr[:, :], row(ctx_k[bass.ds(l * NPAIR + p, 1), :, :])).then_inc(ck_in, 16)
                    g.wait_ge(strip_used, pairs.value() + OPEN)
                    carry(g)
                    g.dma_start(strip[:, :, :], row(strips[bass.ds(l * NPAIR + p, 1), :, :, :])).then_inc(strip_in, 16)
                    g.wait_ge(nkst_ready, pairs.value(1))
                    carry(g)
                    g.dma_start(row(k_out[bass.ds(l * NPAIR + p, 1), :, :]), nkst[:, :]).then_inc(nk_saved, 16)
                    pairs.add()
                g.wait_ge(nvst_ready, lay.value() * 2 + 2)
                carry(g)
                g.dma_start(row(v_out[bass.ds(l, 1), :, :]), nvst[:, :]).then_inc(nv_saved, 16)
                g.wait_ge(merged_ready, lay.value() * 2 * KD + 2 * KD)
                g.wait_ge(x_saved, lay.value() * 16 + 16)
                carry(g)
                g.dma_start(x[:, :, :], x_keep).then_inc(x_back, 16)
                g.wait_ge(ssq_added, lay.value() * 2 * KD + KD + OPEN)
                carry(g)
                with loop(g, FB, {downs: 1}) as i:
                    g.wait_ge(d_lo, downs.value() + OPEN)
                    carry(g)
                    g.dma_start(draw[:, :, :],
                                w_down[bass.ds(l * FB + i, 1), :, :].rearrange("a p (k n) -> (a p) k n", k=2)).then_inc(d_in, 16)
                    downs.add()
                lay.add()
            g.wait_ge(xn_ready, 2 * DEPTH * KD)
            g.dma_start(x_out, x[:, :, :]).then_inc(y_saved, 16)
            g.wait_ge(st_saved, 16 * DEPTH * RH + 16)
            g.wait_ge(nk_saved, 16 * DEPTH * NPAIR + 16)
            g.wait_ge(nv_saved, 16 * DEPTH + 16)
            g.wait_ge(y_saved, 16)

        @block.tensor
        def _(pe):
            U = Units(pe, unit, unit_ready, unit_free)
            S = Slabs()
            lay, ada_n, heads, pairs, sqs, downs, hids = (Tally() for _ in range(7))

            def product(out, a, b, first, last):
                pe.matmul(out, a[0], b[0], start=first, stop=False)
                pe.matmul(out, a[0], b[1], start=False, stop=False)
                return pe.matmul(out, a[1], b[0], start=False, stop=last)

            def linear(w, acts, chunks, wait_chunk=None):
                u = U.take()
                for k in range(chunks):
                    if wait_chunk:
                        wait_chunk(k)
                    a, n, f, z = w(k), HALF, k == 0, k == chunks - 1
                    xs = [[t[:, k, h * n:(h + 1) * n] for t in acts] for h in range(2)]
                    for h in range(2):
                        pe.matmul(u[:, h, 0:n], a[0], xs[h][0], start=f, stop=False)
                        pe.matmul(u[:, h, 0:n], a[0], xs[h][1], start=False, stop=False)
                    for h in range(2):
                        mm = pe.matmul(u[:, h, 0:n], a[1], xs[h][0], start=False, stop=z)
                U.give(mm)

            def slab(cols, chunks, wait=True):
                s_ = S.slot()
                pe.wait_ge(w_lo[s_], S.uses() + 1 + OPEN)
                S.add()
                hi, lo = (t[s_][:, 0:chunks * cols].rearrange("p (k n) -> p k n", k=chunks) for t in (wh, wl))
                return lambda c: (lambda k: (hi[:, k, c * P:(c + 1) * P], lo[:, k, c * P:(c + 1) * P])), hi, lo

            def values():
                _, hi, lo = slab(256, KD)
                for tiles in (range(4), range(4, 5)):
                    u = U.take()
                    for t in tiles:
                        out = u[:, t % 4 // 2, t % 2 * 256:t % 2 * 256 + 256]
                        for k in range(KD):
                            a = [m[:, k, t * P:(t + 1) * P] for m in (hmh, hml)]
                            mm = product(out, a, (hi[:, k, :], lo[:, k, :]), k == 0, k == KD - 1)
                    U.give(mm)

            def stats(sq):
                u = U.take()
                for c in range(KD):
                    pe.wait_ge(sq_ready, sqs.value(c + 1))
                    for h in range(2):
                        mm = pe.matmul(u[:, h, 0:HALF], ones[:, :], sq[:, c % 2, h * HALF:(h + 1) * HALF],
                                       start=c == 0, stop=c == KD - 1)
                    if c < KD - 2:
                        mm.then_inc(sq_used, 1)
                U.give(mm)
                sqs.add(KD)

            def total(ssq, which):
                pe.wait_ge(ssq_added, which + OPEN)
                u = U.take()
                for h in range(2):
                    mm = pe.matmul(u[:, h, 0:HALF], ones[:, :], ssq[:, h * HALF:(h + 1) * HALF], start=True, stop=True)
                U.give(mm)

            pe.wait_ge(const_set, 2)
            wait_constants(pe)
            stats(scratch_b[2])
            pe.wait_ge(cs_ready, 1)
            per_layer = {U: 236, S: MAIN, lay: 1, ada_n: ADA // 4, heads: RH, pairs: NPAIR, sqs: 2 * KD, downs: FB, hids: FB}
            with loop(pe, DEPTH, per_layer) as l:
                with loop(pe, ADA // 4, {ada_n: 1}) as i:
                    for n in range(4):
                        pe.wait_ge(ada_in[n], ada_n.value(1) * 16)
                        for c in range(2):
                            out = tp[0][:, bass.ds(i * 16 + (n * 4 + c * 2), 2)]
                            for k in range(KD):
                                mm = pe.matmul(out, ada[n][:, k, c * P:(c + 1) * P], cs[:, k, :],
                                               start=k == 0, stop=k == KD - 1)
                        mm.then_inc(ada_used, 1)
                    ada_n.add()

                def hm_wait(part):
                    return lambda k: pe.wait_ge(hm_ready, lay.value() * 2 * KD + part * KD + k + 1)

                with loop(pe, RH // 2, {U: 20, S: 6, heads: 2}):
                    for hh in range(2):
                        w, _, _ = slab(256, KD)
                        linear(w(0), (hmh, hml), KD, hm_wait(0) if hh == 0 else None)
                        linear(w(1), (hmh, hml), KD)
                        values()
                        pe.wait_ge(qk_ready, heads.value() * 2 + 2)
                        pe.transpose(tp[0][:, 0:P], ks[:, NS:T], ident[:, :]).then_inc(kt_ready, 1)

                        def score(i):
                            if i >= 2:
                                pe.wait_ge(p_full, heads.value() * 5 + i - 1)
                            n = NS if i < 4 else P
                            keys = [t[:, i * P:(i + 1) * P] for t in (kh, kl)]
                            qrs = [t[:, 0:NS] if i < 4 else t[:, NS:T] for t in (qh, ql)]
                            product(sc[i % 2][:, 0:n], keys, qrs, True, True).then_inc(sc_ready, 1)

                        score(0)
                        score(1)
                        w, _, _ = slab(256, KD)
                        linear(w(0), (hmh, hml), KD)
                        score(2)
                        score(3)
                        linear(w(1), (hmh, hml), KD)
                        score(4)
                        pe.wait_ge(s0_ready, heads.value(1) + OPEN)
                        pe.wait_ge(qd_ready, heads.value(1))
                        for c in range(2):
                            u = U.take()
                            cols = slice(c * P, (c + 1) * P)
                            for i in range(4):
                                if c == 0:
                                    pe.wait_ge(p_ready, heads.value() * 5 + i + 1)
                                product(u[:, 0, :], (vh[:, i, cols], vl[:, i, cols]),
                                        (ph[:, i * NS:(i + 1) * NS], pl[:, i * NS:(i + 1) * NS]), i == 0, False)
                            for d in range(2):
                                product(u[:, 0, :], (s0h[:, d, cols], s0l[:, d, cols]),
                                        (qdh[:, d, :], qdl[:, d, :]), False, d == 1)
                            if c == 0:
                                pe.wait_ge(p_ready, heads.value() * 5 + 5)
                            U.give(product(u[:, 1, 0:P], (vh[:, 4, cols], vl[:, 4, cols]),
                                           (ph[:, 4 * NS:], pl[:, 4 * NS:]), True, True))
                        pe.wait_ge(kz_ready, heads.value(1))
                        for d in range(2):
                            mm = product(tp[1][:, d * DV:(d + 1) * DV], (kzh[:, d, :], kzl[:, d, :]),
                                         (vh[:, 4, :], vl[:, 4, :]), True, True)
                        mm.then_inc(st_psum, 1)
                        U.wait_released(1)
                        u = U.take()
                        for h in range(2):
                            for c in range(2):
                                mm = pe.matmul(u[:, h, 0:HALF], ones[:, :], y[:, c, h * HALF:(h + 1) * HALF],
                                               start=c == 0, stop=c == 1)
                        U.give(mm)
                        pe.wait_ge(ysq_ready, heads.value(1))
                        u = U.take()
                        for h in range(2):
                            for c in range(2):
                                mm = pe.matmul(u[:, h, 0:HALF], ones[:, :], sq2[:, c, h * HALF:(h + 1) * HALF],
                                               start=c == 0, stop=c == 1)
                        U.give(mm)
                        heads.add()
                with loop(pe, KD // 2, {U: 4, S: 2}) as j:
                    w, _, _ = slab(256, KD)
                    linear(w(0), (hmh, hml), KD)
                    linear(w(1), (hmh, hml), KD)
                    w, _, _ = slab(256, KD)
                    linear(w(0), (yrh, yrl), KD, lambda k: pe.wait_ge(yr_ready, lay.value() * KD + k + 1))
                    linear(w(1), (yrh, yrl), KD)
                for _ in range(2):
                    values()
                pe.wait_ge(cv_ready, lay.value(1))
                carry(pe)
                with loop(pe, NPAIR // 2, {U: 8, S: 2, pairs: 2}) as pp:
                    for ph_ in range(2):
                        w, _, _ = slab(256, KD)
                        linear(w(0), (hmh, hml), KD)
                        linear(w(1), (hmh, hml), KD)
                        U.wait_released(2)
                        U.wait_released(1)
                        pe.wait_ge(ck_ready, pairs.value(1) + OPEN)
                        ou = None

                        def score(v):
                            hh, j = divmod(v, 5)
                            if v >= 2:
                                pe.wait_ge(s_ready, pairs.value() * 10 + v - 1)
                            rows = slice(64 * hh, 64 * hh + 64)
                            if j < 4:
                                first, tiles, _ = BLOCKS[j]
                                n = tiles * P
                                q = [t[rows, j * P:(j + 1) * P] for t in (nqh, nql)]
                                product(sc[v % 2][:, 0:n], q, [t[rows, first * P:first * P + n] for t in (nkh, nkl)], True, True)
                                mm = product(sc[v % 2][:, n:n + P], q, [t[rows, :] for t in (ckh, ckl)], True, True)
                            else:
                                mm = product(sc[v % 2][:, 0:P], [t[rows, NS:T] for t in (nqh, nql)],
                                             [t[rows, NS:T] for t in (nkh, nkl)], True, True)
                            mm.then_inc(nsc_ready, 1)

                        def turn(v):
                            n = BLOCKS[v % 5][1] + 1 if v % 5 < 4 else 1
                            pe.wait_ge(e_ready, pairs.value() * 10 + v + 1)
                            if v >= 2:
                                pe.wait_ge(pt_ready, pairs.value() * 10 + v - 1)
                            for i in range(n):
                                mm = pe.transpose(tp[v % 2][:, i * P:(i + 1) * P], s[:, v % 2, i * P:(i + 1) * P], ident[:, :])
                            mm.then_inc(t_ready, 1)

                        def weigh(v, u):
                            hh, j = divmod(v, 5)
                            pe.wait_ge(pt_ready, pairs.value() * 10 + v + 1)
                            out = u[:, 0, j * P + hh * 64:j * P + hh * 64 + 64] if j < 4 else u[:, 1, hh * 64:hh * 64 + 64]
                            tiles = [BLOCKS[j][0] + i for i in range(BLOCKS[j][1])] + ["ctx"] if j < 4 else [4]
                            col = pp * 256 + (ph_ * P + hh * 64)
                            for i, t in enumerate(tiles):
                                if t == "ctx":
                                    vals = [m[:, bass.ds(col, 64)] for m in (cvh, cvl)]
                                else:
                                    vals = [m[:, t, bass.ds(col, 64)] for m in (nvh, nvl)]
                                mm = product(out, [m[:, v % 2, i * P:(i + 1) * P] for m in (pth, ptl)], vals,
                                             i == 0, i == len(tiles) - 1)
                            if v < 9:
                                mm.then_inc(pt_used, 1)
                            return mm

                        for v in range(12):
                            if v < 10:
                                score(v)
                            if 1 <= v < 11:
                                turn(v - 1)
                            if v == 2:
                                ou = U.take()
                            if v >= 2:
                                mm = weigh(v - 2, ou)
                        U.give(mm)
                        U.wait_released(1)
                        u = U.take()
                        for t in range(5):
                            mm = pe.transpose(u[:, t // 4, t % 4 * P:(t % 4 + 1) * P], o[:, t, :], ident[:, :])
                        U.give(mm)
                        pairs.add()
                for J in range(2):
                    for _ in range(2):
                        w, _, _ = slab(256, KD)
                        linear(w(0), (hmh, hml), KD)
                        linear(w(1), (hmh, hml), KD)
                    w, _, _ = slab(512, NPAIR)
                    for c in range(4):
                        linear(w(c), (ynh, ynl), NPAIR,
                               (lambda k: pe.wait_ge(yn_ready, lay.value() * NPAIR + k + 1)) if J == 0 and c == 0 else None)
                with loop(pe, 2, {U: 4, S: 2}):
                    for n in range(2):
                        w, _, _ = slab(256, KD)
                        linear(w(0), (mh, ml), KD, (lambda k: pe.wait_ge(m_ready, lay.value() * KD + k + 1)) if n == 0 else None)
                        linear(w(1), (mh, ml), KD)
                total(scratch_a[0], lay.value() * 2 * KD + KD)
                stats(scratch_a[2])

                def gate_up(first=False):
                    for n in range(2):
                        w, _, _ = slab(256, KD)
                        linear(w(0), (hmh, hml), KD, hm_wait(1) if first and n == 0 else None)
                        linear(w(1), (hmh, hml), KD)

                def down(buf):
                    pe.wait_ge(d_lo, downs.value(1) + OPEN)
                    pe.wait_ge(hid_ready, downs.value(1) * 2)
                    for c in range(KD):
                        linear(lambda k: (dwh[:, k, c * P:(c + 1) * P], dwl[:, k, c * P:(c + 1) * P]),
                               (hidh[:, buf, :, :], hidl[:, buf, :, :]), 2)
                    downs.add()

                gate_up(first=True)
                with loop(pe, (FB - 1) // 2, {U: 24, S: 4, downs: 2}):
                    gate_up()
                    down(0)
                    gate_up()
                    down(1)
                down(0)
                total(scratch_b[0], lay.value() * 2 * KD + 2 * KD)
                stats(scratch_b[2])
                hids.add(FB)
                lay.add()

        @block.scalar
        def _(act):
            U = Units(act, unit, unit_ready, unit_free)
            S = Slabs()
            lay, heads, pairs, sqs, hms, downs, hids, osq = (Tally() for _ in range(8))

            def split():
                U.wait_all_done()
                n = S.slot()
                act.wait_ge(raw_in[n], (S.uses() + 1) * 16)
                act.activation(wh[n][:, :], raw[n][:, :], ACT.Copy).then_inc(w_hi[n], 1)
                S.add()

            def hi_of_unit(out, view, scale=1.0):
                act.activation(out, view, ACT.Copy, scale=scale).then_inc(unit_hi, 1)

            def squares(sq):
                for c in range(KD):
                    if c >= 2:
                        act.wait_ge(sq_used, sqs.value() * 6 + c - 1)
                    yield c
                    act.activation(sq[:, c % 2, :], x[:, c, :], ACT.Square).then_inc(sq_ready, 1)
                sqs.add()

            def root(rstd):
                u = U.get()
                U.release(act.activation(halves(rstd[:, :]), u[:, :, 0:HALF], ACT.Sqrt, bias=epsc[:, 0:1], scale=1.0 / D))

            def modulated(t, f, scale, shift_at):
                for c in range(KD):
                    act.wait_ge(xt_ready, hms.value(c + 1))
                    if c >= 2:
                        act.wait_ge(hm_ready, hms.value(c - 1))
                    for i, cols in STREAMS:
                        sc_, sh_ = scale[:, c, i:i + 1], mod[:, shift_at + c, i:i + 1]
                        act.activation(hmh[:, c, cols], t[:, c % 2, cols], ACT.Identity, bias=sh_, scale=sc_)
                    for i, cols in STREAMS:
                        sc_, sh_ = scale[:, c, i:i + 1], mod[:, shift_at + c, i:i + 1]
                        a = act.activation(f[:, c % 2, cols], t[:, c % 2, cols], ACT.Identity, bias=sh_, scale=sc_)
                    a.then_inc(f_ready, 1)
                hms.add(KD)

            act.wait_ge(const_set, 2)
            act.wait_ge(x_back, 16)
            for c in squares(scratch_b[2]):
                pass
            wait_constants(act)
            act.activation(cs[:, :, :], cv[:, :, :], ACT.Silu).then_inc(cs_ready, 1)
            for n in range(2):
                act.wait_ge(raw_in[n], 16)
                act.activation(wh[n][:, :], raw[n][:, :], ACT.Copy).then_inc(w_hi[n], 1)
                S.add()
            per_layer = {U: 236, S: MAIN, lay: 1, heads: RH, pairs: NPAIR, sqs: 2, hms: 2 * KD, downs: FB, hids: 2 * FB, osq: 2 * KD}
            with loop(act, DEPTH, per_layer) as l:
                act.wait_ge(lg_z, lay.value() * 2 + 1)
                act.activation(lt[:, 0, :], lt[:, 1, :], ACT.Exp, scale=-1.0).then_inc(lg_e, 1)
                root(scratch_b[1])
                act.wait_ge(mod_ready, lay.value(1))
                modulated(scratch_b[2], scratch_b[3], am1, SH1)
                with loop(act, RH // 2, {U: 20, S: 6, heads: 2}):
                    for hh in range(2):
                        act.wait_ge(lgh_ready, heads.value(1))
                        act.activation(dst[:, :], dst[:, :], ACT.Exp)
                        for d in range(2):
                            act.activation(xf[:, d, :], pos[:, d, :], ACT.Exp, scale=lgh[:, d:d + 1])
                        for d in range(2):
                            a = act.activation(zh[:, d:d + 1], zpos[:, d:d + 1], ACT.Exp, scale=lgh[:, d:d + 1])
                        a.then_inc(dexp_ready, 1)
                        for to, scale in ((qs, 1.0), (ks, K_SCALE)):
                            u = U.get()
                            U.release(act.activation(halves(to[:, :]), u[:, :, 0:HALF], ACT.Copy, scale=scale))
                        act.drain()
                        for to, of in ((qsw, qs), (ksw, ks)):
                            act.activation(to[0:64, :], of[64:P, 0:NS], ACT.Copy)
                            act.activation(to[64:P, :], of[0:64, 0:NS], ACT.Copy).then_inc(swap_ready, 1)
                        split()
                        for n, (to, of) in enumerate(((qh, qs), (kh, ks))):
                            act.wait_ge(roped, heads.value() * 2 + n + 1)
                            act.activation(to[:, :], of[:, :], ACT.Copy).then_inc(qk_hi, 1)
                        act.wait_ge(qd_full, heads.value(1))
                        act.activation(qdh[:, 0, :], qsw[:, :], ACT.Copy)
                        act.activation(qdh[:, 1, :], ksw[:, :], ACT.Copy).then_inc(qd_hi, 1)
                        u = U.get()
                        hi_of_unit(vh[:, 0:4, :].rearrange("p (a b) n -> p a (b n)", a=2), u[:, :, :])
                        U.add()
                        u = U.get()
                        hi_of_unit(vh[:, 4, :], u[:, 0, 0:DV])
                        U.add()
                        split()
                        act.wait_ge(s0_in, heads.value(1) * 16)
                        act.activation(s0h[:, :, :], s0r[:, :, :], ACT.Copy).then_inc(s0_hi, 1)
                        act.wait_ge(kt_ready, heads.value(1))
                        act.wait_ge(qd_ready, heads.value(1))
                        for d in range(2):
                            act.activation(kz[:, d, :], tp[0][:, 0:P], ACT.Copy, scale=zh[:, d:d + 1])
                        act.drain()
                        act.activation(kzh[:, :, :], kz[:, :, :], ACT.Copy).then_inc(kz_hi, 1)

                        def p_split(i):
                            act.wait_ge(p_full, heads.value() * 5 + i + 1)
                            n = NS if i < 4 else P
                            act.activation(ph[:, i * NS:i * NS + n], pst[:, i % 2, 0:n], ACT.Copy).then_inc(p_hi, 1)

                        def gate_c(c):
                            u = U.get()
                            U.release(act.activation(halves(sg[:, c, :]), u[:, :, 0:HALF], ACT.Silu))

                        p_split(0)
                        p_split(1)
                        gate_c(0)
                        p_split(2)
                        p_split(3)
                        gate_c(1)
                        split()
                        p_split(4)
                        for c in range(2):
                            u = U.get()
                            act.activation(y[:, c, 0:NS], u[:, 0, :], ACT.Copy)
                            U.release(act.activation(y[:, c, NS:T], u[:, 1, 0:P], ACT.Copy))
                        act.wait_ge(st_psum, heads.value(1))
                        act.wait_ge(st_saved, heads.value() * 16 + 16)
                        act.activation(st[:, :, :], tp[1][:, :].rearrange("p (d n) -> p d n", d=2), ACT.Copy).then_inc(st_ready, 1)
                        U.add()
                        U.wait_released(1)
                        act.activation(sq2[:, :, :], y[:, :, :], ACT.Square).then_inc(ysq_ready, 1)
                        u = U.get()
                        U.release(act.activation(halves(qs[:, :]), u[:, :, 0:HALF], ACT.Sqrt, bias=epsc[:, 0:1], scale=1.0 / DV))
                        heads.add()
                act.wait_ge(yret_ready, heads.value())
                for c in range(KD):
                    act.activation(yrh[:, c, :], yret[:, c, :], ACT.Copy).then_inc(yr_hi, 1)
                with loop(act, KD // 2, {U: 4, S: 2}):
                    for c in range(2):
                        u = U.get()
                        U.release(act.activation(halves(gate[:, c, :]), u[:, :, 0:HALF], ACT.Sigmoid))
                    split()
                    U.add(2)
                    split()
                for n in range(2):
                    cols = slice(n * 256, n * 256 + 256)
                    u = U.get()
                    hi_of_unit(nvh[:, 0:4, cols].rearrange("p (a b) n -> p a b n", a=2), u[:, :, :].rearrange("p a (b n) -> p a b n", b=2))
                    U.add()
                    u = U.get()
                    if n == 0:
                        act.wait_ge(nv_saved, lay.value() * 16 + 16)
                    act.activation(nvst[:, cols], u[:, 0, 0:256], ACT.Copy).then_inc(nvst_ready, 1)
                    hi_of_unit(nvh[:, 4, cols], u[:, 0, 0:256])
                    U.add()
                    split()
                act.wait_ge(cv_in, lay.value(1) * 16)
                act.activation(cvh[:, :], cvr[:, :], ACT.Copy).then_inc(cv_hi, 1)
                with loop(act, NPAIR // 2, {U: 8, S: 2, pairs: 2}) as pp:
                    for ph_ in range(2):
                        for to, scale in ((nqh, -Q_SCALE), (nkh, 1.0)):
                            u = U.get()
                            if scale == 1.0:
                                act.wait_ge(nk_saved, pairs.value() * 16 + 16)
                                act.activation(nkst[:, :], u[:, 1, 192:HALF], ACT.Copy).then_inc(nkst_ready, 1)
                            hi_of_unit(halves(to[:, :]), u[:, :, 0:HALF], scale)
                            U.add()
                        split()
                        act.wait_ge(ck_in, pairs.value(1) * 16)
                        act.activation(ckh[:, :], ckr[:, :], ACT.Copy).then_inc(ck_hi, 1)

                        def width(v):
                            return (BLOCKS[v % 5][1] + 1) * P if v % 5 < 4 else P

                        for v in range(11):
                            if v < 10:
                                n = width(v)
                                act.wait_ge(s_ready, pairs.value() * 10 + v + 1)
                                act.activation(s[:, v % 2, 0:n], s[:, v % 2, 0:n], ACT.Exp, bias=nmax[:, v:v + 1], scale=-1.0,
                                               accum_out=sums[:, v:v + 1]).then_inc(e_ready, 1)
                            if v >= 1:
                                n = width(v - 1)
                                act.wait_ge(t_ready, pairs.value() * 10 + v)
                                if v >= 3:
                                    act.wait_ge(pt_used, pairs.value() * 9 + v - 2)
                                act.activation(pth[:, (v - 1) % 2, 0:n], tp[(v - 1) % 2][:, 0:n], ACT.Copy).then_inc(pt_hi, 1)
                        U.add()
                        u = U.get()
                        own = yna[:, bass.ds(pp * 2 + ph_, 1), :]
                        act.activation(flat(own)[:, NS:T], u[:, 1, 0:P], ACT.Copy)
                        U.release(act.activation(flat(own)[:, 0:NS], u[:, 0, :], ACT.Copy))
                        pairs.add()
                act.drain()
                for c in range(NPAIR):
                    act.activation(ynh[:, c, :], yna[:, c, :], ACT.Copy).then_inc(yn_hi, 1)
                for J in range(2):
                    for n in range(2):
                        for c in range(2):
                            u = U.get()
                            U.release(act.activation(halves(gate4[:, 2 * n + c, :]), u[:, :, 0:HALF], ACT.Sigmoid))
                        split()
                    U.add(4)
                    split()
                act.wait_ge(nk_saved, pairs.value() * 16 + 16)
                act.wait_ge(nv_saved, lay.value(1) * 16 + 16)
                for c in range(KD):
                    act.wait_ge(merged_ready, lay.value() * 2 * KD + KD + c + 1)
                    act.activation(mh[:, c, :], merged[:, c, :], ACT.Copy).then_inc(m_hi, 1)
                act.wait_ge(m_ready, lay.value() * KD + KD)
                with loop(act, 2, {U: 4, S: 2, osq: 4}) as i:
                    for n in range(4):
                        u = U.get()
                        if n >= 2:
                            act.wait_ge(ssq_added, osq.value(n - 1) + OPEN)
                        elif n == 0:
                            act.wait_ge(ssq_added, osq.value() + OPEN)
                        act.activation(halves(scratch_a[2][:, n % 2, :]), u[:, :, 0:HALF], ACT.Square).then_inc(osq_ready, 1)
                        g_ = gm1[:, bass.ds(i * 4 + n, 1), :]
                        o_ = flat(mix[:, bass.ds(i * 4 + n, 1), :])
                        act.activation(o_[:, 0:HALF], u[:, 0, 0:HALF], ACT.Copy, scale=flat(g_)[:, 0:1])
                        act.activation(o_[:, HALF:NS], u[:, 1, 0:NS - HALF], ACT.Copy, scale=flat(g_)[:, 0:1])
                        U.release(act.activation(o_[:, NS:T], u[:, 1, NS - HALF:HALF], ACT.Copy, scale=flat(g_)[:, 1:2]))
                        if n % 2:
                            split()
                    osq.add(4)
                root(scratch_a[1])
                for c in squares(scratch_a[2]):
                    act.wait_ge(xn_ready, lay.value() * 2 * KD + c + 1)
                root(scratch_a[1])
                modulated(scratch_a[2], scratch_a[3], am2, SH2)

                def gate_up(buf):
                    for n in range(2):
                        u = U.get()
                        U.release(act.activation(halves(sig[:, :]), u[:, :, 0:HALF], ACT.Silu))
                        U.add()
                        U.wait_released(1)
                        act.activation(hidh[:, buf, n, :], hid[:, :], ACT.Copy).then_inc(hid_hi, 1)
                        split()

                def down_split():
                    U.wait_all_done()
                    act.wait_ge(d_in, downs.value(1) * 16)
                    act.activation(dwh[:, :, :], draw[:, :, :], ACT.Copy).then_inc(d_hi, 1)
                    downs.add()

                gate_up(0)
                down_split()
                with loop(act, (FB - 1) // 2, {U: 24, S: 4, downs: 2}):
                    for buf in (1, 0):
                        gate_up(buf)
                        U.add(KD)
                        down_split()
                for c in range(KD):
                    U.add()
                    U.wait_released(1)
                    if c >= 2:
                        act.wait_ge(ssq_added, osq.value(c - 1) + OPEN)
                    act.activation(scratch_b[2][:, c % 2, :], mix[:, c, :], ACT.Square).then_inc(osq_ready, 1)
                    act.drain()
                    for i, cols in STREAMS:
                        a = act.activation(mix[:, c, cols], mix[:, c, cols], ACT.Copy, scale=gm2[:, c, i:i + 1])
                    a.then_inc(accg_ready, 1)
                osq.add(KD)
                root(scratch_b[1])
                for c in squares(scratch_b[2]):
                    act.wait_ge(xn_ready, lay.value() * 2 * KD + KD + c + 1)
                hids.add(2 * FB)
                lay.add()

        @block.vector
        def _(dve):
            U = Units(dve, unit, unit_ready, unit_free)
            S = Slabs()
            lay, heads, pairs, hms, downs, hids, osq, his = (Tally() for _ in range(8))

            def split():
                n = S.slot()
                dve.wait_ge(w_hi[n], S.uses() + 1)
                dve.tensor_tensor(wl[n][:, :], raw[n][:, :], f32(wh[n][:, :]), ALU.subtract).then_inc(w_lo[n], 1)
                S.add()

            def lo(out, full, hi):
                return dve.tensor_tensor(out, full, f32(hi), ALU.subtract)

            def wait_hi():
                his.add()
                dve.wait_ge(unit_hi, his.value())

            def inverse_root(rstd):
                U.add()
                U.wait_released(1)
                dve.reciprocal(rstd[:, :], rstd[:, :])
                dve.drain()

            def modulate(t, f, rstd):
                for c in range(KD + 1):
                    if c < KD:
                        if c >= 2:
                            dve.wait_ge(f_ready, hms.value(c - 1))
                        dve.tensor_tensor(t[:, c % 2, :], x[:, c, :], rstd[:, :], ALU.mult).then_inc(xt_ready, 1)
                    if c >= 1:
                        dve.wait_ge(f_ready, hms.value(c))
                        lo(hml[:, c - 1, :], f[:, (c - 1) % 2, :], hmh[:, c - 1, :]).then_inc(hm_ready, 1)
                hms.add(KD)

            def residual(rstd, ready):
                for c in range(0, KD, 2):
                    for n in range(2):
                        dve.tensor_tensor(mix[:, c + n, :], mix[:, c + n, :], rstd[:, :], ALU.mult)
                    dve.drain()
                    for n in range(2):
                        dve.tensor_tensor(x[:, c + n, :], x[:, c + n, :], mix[:, c + n, :], ALU.add).then_inc(xn_ready, 1)

            def sum_squares(sq, ssq, n):
                for c in range(n):
                    dve.drain()
                    dve.wait_ge(osq_ready, osq.value(c + 1))
                    dve.tensor_tensor(ssq[:, :], ssq[:, :], sq[:, c % 2, :], ALU.add).then_inc(ssq_added, 1)
                osq.add(n)

            def layer_constants(l):
                dve.tensor_copy(par[:, :], flat(par_all[:, bass.ds(l, 1), :]))
                dve.tensor_copy(lt[:, 5, :], flat(decay_all[:, bass.ds(l, 1), :]))
                dve.drain()
                dve.tensor_scalar(lt[:, 2, :], lt[:, 5, :], -1.0, None, ALU.mult)
                dve.drain()
                dve.tensor_tensor(lt[:, 1, :], lt[:, 5, :], lt[:, 2, :], ALU.max).then_inc(lg_z, 1)
                dve.wait_ge(lg_e, lay.value(1))
                dve.tensor_scalar(lt[:, 2, :], lt[:, 0, :], 2.0, None, ALU.add)
                dve.drain()
                dve.reciprocal(lt[:, 2, :], lt[:, 2, :])
                dve.drain()
                dve.tensor_tensor(lt[:, 2, :], lt[:, 0, :], lt[:, 2, :], ALU.mult)
                dve.drain()
                dve.tensor_tensor(lt[:, 3, :], lt[:, 2, :], lt[:, 2, :], ALU.mult)
                dve.drain()
                dve.tensor_scalar(lt[:, 4, :], lt[:, 3, :], 1.0 / 15, None, ALU.mult)
                for n in (13, 11, 9, 7, 5, 3):
                    dve.drain()
                    dve.scalar_tensor_tensor(out=lt[:, 4, :], in0=lt[:, 4, :], scalar=1.0 / n, in1=lt[:, 3, :], op0=ALU.add, op1=ALU.mult)
                dve.drain()
                dve.scalar_tensor_tensor(out=lt[:, 4, :], in0=lt[:, 4, :], scalar=1.0, in1=lt[:, 2, :], op0=ALU.add, op1=ALU.mult)
                dve.tensor_scalar(lt[:, 5, :], lt[:, 5, :], 0.0, None, ALU.min)
                dve.drain()
                dve.scalar_tensor_tensor(out=lg[:, :], in0=lt[:, 4, :], scalar=-2.0, in1=lt[:, 5, :], op0=ALU.mult, op1=ALU.add)\
                   .then_inc(lg_z, 1)
                dve.wait_ge(ada_used, lay.value(1) * ADA + OPEN)
                n = 6 * KD
                dve.tensor_tensor(mod[:, :, :], tp[0][:, 0:2 * n].rearrange("p (c s) -> p c s", s=2),
                                  par[:, B_ADA:B_ADA + n].unsqueeze(2).broadcast_to([P, n, 2]), ALU.add)
                dve.drain()
                for out, part, gain, plus in ((am1, SC1, N_PRE_MIX, 1.0), (gm1, G1, N_POST_MIX, 0.0),
                                              (am2, SC2, N_PRE_FFN, 1.0), (gm2, G2, N_POST_FFN, 0.0)):
                    a = dve.scalar_tensor_tensor(out=out[:, :, :], in0=mod[:, part:part + KD, :], scalar=plus,
                                                 in1=par[:, gain:gain + KD].unsqueeze(2).broadcast_to([P, KD, 2]),
                                                 op0=ALU.add, op1=ALU.mult)
                a.then_inc(mod_ready, 1)

            wait_constants(dve)
            split()
            split()
            per_layer = {U: 236, S: MAIN, lay: 1, heads: RH, pairs: NPAIR, hms: 2 * KD, downs: FB, hids: 2 * FB,
                         osq: 2 * KD, his: 2 * RH + 4 + 2 * NPAIR}
            with loop(dve, DEPTH, per_layer) as l:
                layer_constants(l)
                inverse_root(scratch_b[1])
                modulate(scratch_b[2], scratch_b[3], scratch_b[1])
                with loop(dve, RH // 2, {U: 20, S: 6, heads: 2, his: 4}) as hp:
                    for hh in range(2):
                        head = hp * 2 + hh
                        dve.drain()
                        dve.tensor_copy(lgh[:, 0:1], lg[:, bass.ds(head, 1)])
                        dve.tensor_copy(gainh[:, :], par[:, bass.ds(head * 2 + GN, 2)])
                        dve.tensor_copy(lgh[:, 1:2], lg[:, bass.ds(head + RH, 1)])
                        dve.drain()
                        dve.tensor_scalar(lgh[:, 2:3], lgh[:, 1:2], -1.0, None, ALU.mult)
                        dve.drain()
                        dve.tensor_scalar(dst[:, :], rel[:, :], lgh[:, 2:3], None, ALU.mult)
                        dve.drain()
                        dve.scalar_tensor_tensor(out=dst[:, :], in0=rel[:, :], scalar=lgh[:, 0:1], in1=dst[:, :],
                                                 op0=ALU.mult, op1=ALU.min).then_inc(lgh_ready, 1)
                        dve.wait_ge(dexp_ready, heads.value(1))
                        for at_ in (DIAG, CTX_DIAG):
                            dve.tensor_tensor(dst[:, at_:at_ + P], dst[:, at_:at_ + P], ident[:, :], ALU.add)
                        U.add(2)
                        for n, (a, b) in enumerate(((qs, qsw), (ks, ksw))):
                            dve.wait_ge(swap_ready, heads.value() * 2 + n + 1)
                            dve.tensor_tensor(a[:, 0:NS], a[:, 0:NS], rope[:, 0, :], ALU.mult)
                            dve.tensor_tensor(b[:, :], b[:, :], rope[:, 1, :], ALU.mult)
                            dve.drain()
                            dve.tensor_tensor(a[:, 0:NS], a[:, 0:NS], b[:, :], ALU.add).then_inc(roped, 1)
                        split()
                        for n, (to, of, hi) in enumerate(((ql, qs, qh), (kl, ks, kh))):
                            dve.wait_ge(qk_hi, heads.value() * 2 + n + 1)
                            lo(to[:, :], of[:, :], hi[:, :]).then_inc(qk_ready, 1)
                        dve.tensor_tensor(qsw[:, :], qs[:, 0:NS], xf[:, 0, :], ALU.mult)
                        dve.tensor_tensor(ksw[:, :], qs[:, 0:NS], xf[:, 1, :], ALU.mult).then_inc(qd_full, 1)
                        dve.wait_ge(qd_hi, heads.value(1))
                        lo(qdl[:, 0, :], qsw[:, :], qdh[:, 0, :])
                        lo(qdl[:, 1, :], ksw[:, :], qdh[:, 1, :]).then_inc(qd_ready, 1)
                        wait_hi()
                        u = U.get()
                        U.release(lo(vl[:, 0:4, :].rearrange("p (a b) n -> p a (b n)", a=2), u[:, :, :],
                                     vh[:, 0:4, :].rearrange("p (a b) n -> p a (b n)", a=2)))
                        wait_hi()
                        u = U.get()
                        U.release(lo(vl[:, 4, :], u[:, 0, 0:DV], vh[:, 4, :]))
                        split()
                        dve.wait_ge(s0_hi, heads.value(1))
                        lo(s0l[:, :, :], s0r[:, :, :], s0h[:, :, :]).then_inc(s0_ready, 1)

                        def decay_(i):
                            dve.wait_ge(sc_ready, heads.value() * 5 + i + 1)
                            n, at_ = (NS, DIAG - P * i) if i < 4 else (P, CTX_DIAG)
                            dve.tensor_tensor(pst[:, i % 2, 0:n], sc[i % 2][:, 0:n], dst[:, at_:at_ + n], ALU.mult)\
                               .then_inc(p_full, 1)

                        def p_lo(i):
                            n = NS if i < 4 else P
                            dve.wait_ge(p_hi, heads.value() * 5 + i + 1)
                            lo(pl[:, i * NS:i * NS + n], pst[:, i % 2, 0:n], ph[:, i * NS:i * NS + n]).then_inc(p_ready, 1)

                        decay_(0)
                        decay_(1)
                        dve.wait_ge(kz_hi, heads.value(1))
                        lo(kzl[:, :, :], kz[:, :, :], kzh[:, :, :]).then_inc(kz_ready, 1)
                        p_lo(0)
                        p_lo(1)
                        dve.drain()
                        decay_(2)
                        decay_(3)
                        p_lo(2)
                        p_lo(3)
                        split()
                        dve.drain()
                        decay_(4)
                        p_lo(4)
                        U.add(4)
                        u = U.get()
                        for c in range(2):
                            a = dve.scalar_tensor_tensor(out=halves(y[:, c, :]), in0=u[:, :, 0:HALF], scalar=-1.0 / DV,
                                                         in1=halves(y[:, c, :]), op0=ALU.mult, op1=ALU.add)
                        U.release(a)
                        inverse_root(qs)
                        dve.tensor_tensor(y[:, :, :], y[:, :, :], qs[:, :].unsqueeze(1).broadcast_to([P, 2, T]), ALU.mult)
                        dve.drain()
                        if hh == 0:
                            dve.wait_ge(x_saved, lay.value(1) * 16)
                        for c in range(2):
                            a = dve.scalar_tensor_tensor(out=flat(yret[:, bass.ds(head * 2 + c, 1), :]), in0=y[:, c, :],
                                                         scalar=gainh[:, c:c + 1], in1=sg[:, c, :], op0=ALU.mult, op1=ALU.mult)
                        a.then_inc(yret_ready, 1)
                        heads.add()
                dve.drain()
                dve.wait_ge(st_saved, heads.value() * 16 + 16)
                for c in range(KD):
                    dve.wait_ge(yr_hi, lay.value() * KD + c + 1)
                    lo(yrl[:, c, :], yret[:, c, :], yrh[:, c, :]).then_inc(yr_ready, 1)
                with loop(dve, KD // 2, {U: 4, S: 2}) as j:
                    U.add(2)
                    split()
                    for c in range(2):
                        u = U.get()
                        U.wait_released(2)
                        a = dve.tensor_tensor(flat(merged[:, bass.ds(j * 2 + c, 1), :]).rearrange("p (a b) -> p a b", a=2),
                                              u[:, :, 0:HALF], halves(gate[:, c, :]), ALU.mult)
                        U.release(a)
                    split()
                dve.drain()
                for k_, at_ in enumerate(KIND_AT):
                    a = dve.memset(bias[:, at_ + KIND_W[k_]:at_ + KIND_W[k_] + P], 0.0)
                a.then_inc(merged_ready, KD)
                for n in range(2):
                    cols = slice(n * 256, n * 256 + 256)
                    wait_hi()
                    u = U.get()
                    U.release(lo(nvl[:, 0:4, cols].rearrange("p (a b) n -> p a b n", a=2),
                                 u[:, :, :].rearrange("p a (b n) -> p a b n", b=2),
                                 nvh[:, 0:4, cols].rearrange("p (a b) n -> p a b n", a=2)))
                    wait_hi()
                    u = U.get()
                    U.release(lo(nvl[:, 4, cols], u[:, 0, 0:256], nvh[:, 4, cols]))
                    split()
                dve.wait_ge(cv_hi, lay.value(1))
                lo(cvl[:, :], cvr[:, :], cvh[:, :]).then_inc(cv_ready, 1)
                with loop(dve, NPAIR // 2, {U: 8, S: 2, pairs: 2, his: 4}):
                    for _ in range(2):
                        for to, hi, scale in ((nql, nqh, -Q_SCALE), (nkl, nkh, 1.0)):
                            u = U.get()
                            wait_hi()
                            U.release(dve.scalar_tensor_tensor(out=halves(to[:, :]), in0=u[:, :, 0:HALF], scalar=scale,
                                                               in1=f32(halves(hi[:, :])), op0=ALU.mult, op1=ALU.subtract))
                        split()
                        dve.wait_ge(ck_hi, pairs.value(1))
                        lo(ckl[:, :], ckr[:, :], ckh[:, :]).then_inc(ck_ready, 1)
                        for v in range(11):
                            if v in (0, 5):
                                dve.drain()
                                if v == 0:
                                    dve.wait_ge(strip_in, pairs.value(1) * 16)
                                for kind in range(3):
                                    n = KIND_W[kind]
                                    a = dve.scalar_tensor_tensor(
                                        out=bias[:, KIND_AT[kind]:KIND_AT[kind] + n], in0=mask[:, MASK_AT[kind]:MASK_AT[kind] + n],
                                        scalar=BIG, in1=strip[:, v // 5, STRIP_AT[kind]:STRIP_AT[kind] + n],
                                        op0=ALU.mult, op1=ALU.subtract)
                                if v == 5:
                                    a.then_inc(strip_used, 1)
                                dve.drain()
                            if v < 10:
                                j = v % 5
                                if j < 4:
                                    at_, n = KIND_AT[BLOCKS[j][2]], KIND_W[BLOCKS[j][2]] + P
                                else:
                                    at_, n = KIND_W[0], P
                                dve.wait_ge(nsc_ready, pairs.value() * 10 + v + 1)
                                if v >= 2:
                                    dve.wait_ge(t_ready, pairs.value() * 10 + v - 1)
                                carry(dve)
                                dve.tensor_tensor_reduce(s[:, v % 2, 0:n], sc[v % 2][:, 0:n], bias[:, at_:at_ + n], 1.0, 3e38,
                                                         ALU.add, ALU.min, nmax[:, v:v + 1]).then_inc(s_ready, 1)
                            if v >= 1:
                                j = (v - 1) % 5
                                n = KIND_W[BLOCKS[j][2]] + P if j < 4 else P
                                dve.wait_ge(pt_hi, pairs.value() * 10 + v)
                                lo(ptl[:, (v - 1) % 2, 0:n], tp[(v - 1) % 2][:, 0:n], pth[:, (v - 1) % 2, 0:n]).then_inc(pt_ready, 1)
                        dve.reciprocal(rsum[:, :], sums[:, :])
                        dve.drain()
                        u = U.get()
                        rs = rsum[:, :].rearrange("p (h j) -> p j h", h=2)
                        dve.tensor_tensor(o[:, 0:4, :].rearrange("p j (h n) -> p j h n", h=2),
                                          u[:, 0, :].rearrange("p (j h n) -> p j h n", j=4, h=2),
                                          rs[:, 0:4, :].unsqueeze(3).broadcast_to([P, 4, 2, 64]), ALU.mult)
                        U.release(dve.tensor_tensor(o[:, 4, :].rearrange("p (h n) -> p h n", h=2),
                                                    u[:, 1, 0:P].rearrange("p (h n) -> p h n", h=2),
                                                    rs[:, 4, :].unsqueeze(2).broadcast_to([P, 2, 64]), ALU.mult))
                        U.add()
                        pairs.add()
                for c in range(NPAIR):
                    dve.wait_ge(yn_hi, lay.value() * NPAIR + c + 1)
                    lo(ynl[:, c, :], yna[:, c, :], ynh[:, c, :]).then_inc(yn_ready, 1)
                for J in range(2):
                    for n in range(2):
                        U.add(2)
                        split()
                    for c in range(4):
                        dve.drain()
                        u = U.get()
                        U.wait_released(4)
                        U.release(dve.tensor_tensor(halves(mtmp[:, :]), u[:, :, 0:HALF], halves(gate4[:, c, :]), ALU.mult))
                        dve.drain()
                        dve.tensor_tensor(merged[:, J * 4 + c, :], merged[:, J * 4 + c, :], mtmp[:, :], ALU.add)\
                           .then_inc(merged_ready, 1)
                    split()
                dve.wait_ge(nk_saved, pairs.value() * 16 + 16)
                dve.wait_ge(nv_saved, lay.value(1) * 16 + 16)
                for c in range(KD):
                    dve.wait_ge(m_hi, lay.value() * KD + c + 1)
                    lo(ml[:, c, :], merged[:, c, :], mh[:, c, :]).then_inc(m_ready, 1)
                dve.memset(scratch_a[0][:, :], 0.0)
                with loop(dve, 2, {U: 4, S: 2, osq: 4}):
                    for n in range(2):
                        U.add(2)
                        sum_squares(scratch_a[2], scratch_a[0], 2)
                        split()
                inverse_root(scratch_a[1])
                dve.wait_ge(x_back, (lay.value() + 2) * 16)
                residual(scratch_a[1], 0)
                inverse_root(scratch_a[1])
                modulate(scratch_a[2], scratch_a[3], scratch_a[1])

                def gate_up(buf):
                    for n in range(2):
                        U.add()
                        dve.drain()
                        u = U.get()
                        U.wait_released(1)
                        U.release(dve.tensor_tensor(halves(hid[:, :]), u[:, :, 0:HALF], halves(sig[:, :]), ALU.mult))
                        hids.add()
                        dve.wait_ge(hid_hi, hids.value())
                        lo(hidl[:, buf, n, :], hid[:, :], hidh[:, buf, n, :]).then_inc(hid_ready, 1)
                        split()

                def down_split():
                    downs.add()
                    dve.wait_ge(d_hi, downs.value())
                    lo(dwl[:, :, :], draw[:, :, :], dwh[:, :, :]).then_inc(d_lo, 1)

                def down(first=False):
                    dve.drain()
                    for c in range(KD):
                        u = U.get()
                        if first is True:
                            a = dve.tensor_copy(halves(mix[:, c, :]), u[:, :, 0:HALF])
                        else:
                            a = dve.tensor_tensor(halves(mix[:, c, :]), u[:, :, 0:HALF], halves(mix[:, c, :]), ALU.add)
                        U.release(a)

                gate_up(0)
                for c in range(KD):
                    a = dve.memset(mix[:, c, :], 0.0)
                dve.memset(scratch_b[0][:, :], 0.0)
                down_split()
                with loop(dve, (FB - 1) // 2, {U: 24, S: 4, downs: 2, hids: 4}):
                    for buf in (1, 0):
                        gate_up(buf)
                        down()
                        down_split()
                down()
                sum_squares(scratch_b[2], scratch_b[0], KD)
                inverse_root(scratch_b[1])
                dve.wait_ge(accg_ready, lay.value(1) * KD + OPEN)
                residual(scratch_b[1], 1)
                lay.add()


def slabs_of(w, cols):
    K, N = w.shape
    return w.reshape(K // P, P, N // cols, cols).transpose(2, 1, 0, 3).reshape(N // cols, P, K // P * cols)


def feature_major(v):
    return np.swapaxes(v.reshape(*v.shape[:-1], KD, P), -1, -2)


def main_slabs(w_in, w_gate, w_ret_out, w_na_out, w_o, w_fg, w_fu):
    q, k, v, g, nq, nk, nv = np.split(w_in, np.cumsum([512, 512, 1024, 1024, 512, 512]), axis=1)
    parts = []
    for h in range(RH):
        a, b = slice(h * P, (h + 1) * P), slice(h * DV, (h + 1) * DV)
        parts += [slabs_of(np.concatenate([q[:, a], k[:, a]], 1), 256), slabs_of(v[:, b], 256), slabs_of(g[:, b], 256)]
    for j in range(4):
        c = slice(j * 256, (j + 1) * 256)
        parts += [slabs_of(w_gate[:, :D][:, c], 256), slabs_of(w_ret_out[:, c], 256)]
    parts.append(slabs_of(nv, 256))
    for p in range(NPAIR):
        c = slice(p * P, (p + 1) * P)
        parts.append(slabs_of(np.concatenate([nq[:, c], nk[:, c]], 1), 256))
    for J in range(2):
        c = slice(J * 512, (J + 1) * 512)
        parts += [slabs_of(w_gate[:, D:][:, c], 256), slabs_of(w_na_out[:, c], 512)]
    parts.append(slabs_of(w_o, 256))
    for i in range(DFF // P):
        c = slice(i * P, (i + 1) * P)
        parts.append(slabs_of(np.concatenate([w_fg[:, c], w_fu[:, c]], 1), 256))
    return np.concatenate(parts, 0)


def window_strips(rpb):
    c, r, u, rk = np.ogrid[0:16, 0:GR, 0:48, 0:GR]
    dc, dr = np.broadcast_arrays(u - 16 - c + 15, rk - r + 7)
    ok = (dc >= 0) & (dc < 31)
    padded = np.pad(rpb, ((0, 0), (0, 0), (0, 0), (0, 1)))
    return padded[:, :, dr, np.where(ok, dc, 31)].reshape(rpb.shape[0] * NPAIR, 2, P, 384).transpose(0, 2, 1, 3)


def constants():
    t = np.arange(NS)
    t = t % GR * GW + t // GR
    inv = 10000.0 ** (-np.arange(32, dtype=np.float32) / 32)
    ang = np.concatenate([(t // GW).astype(np.float32)[:, None] * inv, (t % GW).astype(np.float32)[:, None] * inv], 1).T
    cos, sin = np.cos(ang), np.sin(ang)
    rope = np.stack([np.concatenate([cos, cos]), np.concatenate([-sin, sin])], 1).astype(np.float32)
    p, i, j = np.arange(P)[:, None], np.arange(P)[None, :], np.arange(CTX_DIAG)[None, :]
    rel = np.concatenate([(j % GR - p % GR) * GW + (j // GR - DIAG // GR) - p // GR, i - p], 1).astype(np.float16)
    pos = np.broadcast_to(np.stack([t + 1, NS - t])[None], (P, 2, NS)).astype(np.float16)
    zpos = np.concatenate([P - 1 - p, p], 1).astype(np.float32)
    masks = []
    for b, u0 in ((0, 16), (1, 0), (3, 0)):
        c = 16 * b + np.arange(16)[:, None, None, None]
        n = 384 if b == 1 else 256
        key = 16 * b - 16 + u0 + np.arange(n // GR)[None, None, :, None]
        start = np.clip(c - WIN // 2, 0, GW - WIN)
        m = np.where((key >= start) & (key < start + WIN), 0, 1)
        masks.append(np.broadcast_to(m, (16, GR, n // GR, GR)).reshape(P, n))
    mask = np.concatenate(masks, 1).astype(np.float16)
    return dict(rope=rope, rel=rel, pos=pos, mask=mask, zpos=zpos, ident=np.eye(P, dtype=np.float32))


def kernel(**inputs):
    import concourse.bacc as bacc
    from concourse.bass_utils import run_bass_kernel_spmd

    v = {k: np.asarray(a) for k, a in inputs.items()}
    arrays = {}
    by_column = v["x_sample"][0].reshape(GR, GW, D).transpose(1, 0, 2).reshape(NS, D)
    arrays["x"] = np.concatenate([by_column, v["x_prompt"][0]], 0).T.reshape(KD, P, T).transpose(1, 0, 2)
    mains = [main_slabs(*(v[n][l] for n in ("w_in", "w_gate", "w_ret_out", "w_na_out", "w_o", "w_ffn_gate", "w_ffn_up")))
             for l in range(DEPTH)]
    arrays["w_main"] = np.concatenate(mains + [mains[0][:2]], 0)
    arrays["w_down"] = v["w_ffn_down"].reshape(DEPTH * FB, 2, P, D).transpose(0, 2, 1, 3).reshape(DEPTH * FB, P, 2 * D)
    arrays["w_ada"] = np.concatenate([slabs_of(v["w_ada"][l], 256) for l in range(DEPTH)], 0)
    arrays["params"] = np.concatenate(
        [feature_major(v[n]) for n in ("norm_pre_mix", "norm_post_mix", "norm_pre_ffn", "norm_post_ffn", "ret_gn_gain")]
        + [v["b_ada"].reshape(DEPTH, 6 * KD, P).transpose(0, 2, 1)], -1).transpose(1, 0, 2)
    arrays["decay"] = np.broadcast_to(v["ret_decay_logit"].reshape(1, DEPTH, 2 * RH), (P, DEPTH, 2 * RH))
    arrays["state"] = v["state_ret"][0].transpose(0, 2, 3, 1, 4).reshape(DEPTH * RH, P, 2, DV)
    arrays["ctx_k"] = v["cache_na_k"][0].transpose(0, 2, 3, 1).reshape(DEPTH * NPAIR, P, P)
    arrays["ctx_v"] = v["cache_na_v"][0].reshape(DEPTH, P, NS)
    arrays["strips"] = window_strips(v["na_rpb"])
    arrays["cvec"] = np.stack([feature_major(v["c"][0]), feature_major(v["c_ctx"])], -1)
    arrays.update(constants())
    outs = {"x_out": (P, KD, T), "k_out": (DEPTH * NPAIR, P, P), "v_out": (DEPTH, P, NS), "state_out": (DEPTH * RH, P, 2, DV)}

    nc = bacc.Bacc("TRN2", target_bir_lowering=False, num_devices=1)
    args = []
    for name in list(arrays):
        arrays[name] = np.ascontiguousarray(arrays[name])
        args.append(nc.dram_tensor(name, arrays[name].shape, mybir.dt.from_np(arrays[name].dtype), kind="ExternalInput").ap())
    args += [nc.dram_tensor(name, shape, F32, kind="ExternalOutput").ap() for name, shape in outs.items()]
    args.append(nc.dram_tensor("x_keep", (P, KD, T), F32, kind="Internal").ap())
    build(nc, *args)
    r = run_bass_kernel_spmd(nc, [arrays], core_ids=[0]).results[0]
    x = r["x_out"].transpose(2, 1, 0).reshape(T, D)
    k = r["k_out"].reshape(1, DEPTH, NPAIR * 2, 64, P).transpose(0, 1, 4, 2, 3)
    vv = r["v_out"].reshape(1, DEPTH, P, NPAIR * 2, 64)
    st = r["state_out"].reshape(1, DEPTH, RH, P, 2, DV).transpose(0, 1, 4, 2, 3, 5)
    latent = x[:NS].reshape(GW, GR, D).transpose(1, 0, 2).reshape(1, NS, D)
    return (x[None, NS:], latent, k, vv, st)
```

```python
from contextlib import ExitStack, contextmanager

import numpy as np

import concourse.bass as bass
from concourse import mybir

P = 128
D = 1024
KD = D // P
NS, NP_ = 512, 128
T = NS + NP_
HALF = T // 2
DEPTH = 2
RH, DV = 4, 256
NPAIR = 4
GW, GR = 64, 8
WIN = 16
DFF = 2816
FB = DFF // 256
SLAB = 2048
ADA_A, ADA_B = 2 * KD, 4 * KD
ADA = ADA_A + ADA_B
RING = 4
MAIN = 58
NPAR = 5 * KD + 6 * KD
EPS = 1e-6
OPEN = 1
K_SCALE = P ** -0.5
Q_SCALE = 64 ** -0.5
BIG = 1e30

F32 = mybir.dt.float32
F32R = mybir.dt.float32r
F16 = mybir.dt.float16
ACT = mybir.ActivationFunctionType
ALU = mybir.AluOpType

N_PRE_MIX, N_POST_MIX, N_PRE_FFN, N_POST_FFN, GN, B_ADA = (KD * i for i in range(6))
SH1, SC1, G1, SH2, SC2, G2 = (KD * i for i in range(6))

BLOCKS = [(0, 2, 0), (0, 3, 1), (1, 3, 1), (2, 2, 2)]
KIND_W = [256, 384, 256]
KIND_AT = [0, 384, 896]
STRIP_AT = [128, 0, 0]
MASK_AT = [0, 256, 640]
BIASW = 1280
DIAG, CTX_DIAG = 384, 896
RELW = 2 * NS


class Tally:

    def __init__(self, step=1):
        self.step, self.count, self.loops = step, 0, []

    def add(self, n=1):
        self.count += n * self.step

    def value(self, more=0):
        v = self.count + more * self.step
        for i, per in self.loops:
            v = i * per + v
        return v


class Units(Tally):

    def __init__(self, eng, tiles, ready, free):
        super().__init__()
        self.eng, self.tiles, self.ready, self.free = eng, tiles, ready, free

    def uses(self, back=0):
        v = (self.count - back) // 2
        for i, per in self.loops:
            assert per % 2 == 0
            v = i * (per // 2) + v
        return v

    def tile(self, back=0):
        return self.tiles[(self.count - back) % 2]

    def take(self):
        self.eng.wait_ge(self.free[self.count % 2], self.uses() + OPEN)
        return self.tile()

    def give(self, instruction):
        instruction.then_inc(self.ready, 1)
        self.add()

    def get(self):
        self.eng.wait_ge(self.ready, self.value(1))
        return self.tile()

    def release(self, instruction):
        instruction.then_inc(self.free[self.count % 2], 1)
        self.add()

    def wait_all_done(self):
        self.eng.wait_ge(self.ready, self.value())

    def wait_released(self, back):
        self.eng.wait_ge(self.free[(self.count - back) % 2], self.uses(back) + 1 + OPEN)


class Slabs(Tally):

    def slot(self):
        return self.count % 2

    def uses(self):
        v = self.count // 2
        for i, per in self.loops:
            assert per % 2 == 0
            v = i * (per // 2) + v
        return v


@contextmanager
def loop(eng, trips, tallies):
    before = {t: t.count for t in tallies}
    with eng.Fori(0, trips) as i:
        for t, per in tallies.items():
            t.loops.append((i, per * t.step))
        yield i
    for t, per in tallies.items():
        assert t.count - before[t] == per * t.step, (per, (t.count - before[t]) / t.step)
        t.loops.pop()
        t.count = before[t] + trips * per * t.step


def build(nc, x_in, w_main, w_down, w_ada, params, decay, state_in, ctx_k, ctx_v, strips, cvec,
          rope_in, rel_in, pos_in, mask_in, zpos_in, ident_in,
          x_out, k_out, v_out, state_out, x_keep):
    ctx = ExitStack()
    with ctx:
        arena0 = -(-nc.sbuf_base // 32) * 32
        room = nc.sbuf_usable_end - arena0
        nc.alloc_sbuf_tensor("arena", [P, (room - 64) // 4], F32)
        top = [0]

        def at(name, shape, offset, dt=F32):
            return nc.alloc_sbuf_tensor_at(name, shape, dt, offset=arena0 + offset)

        def fixed(name, shape, dt=F32):
            n = int(np.prod(shape[1:])) * (2 if dt == F16 else 4)
            t = at(name, shape, top[0], dt)
            top[0] += -(-n // 32) * 32
            return t

        def sem(name):
            return ctx.enter_context(nc.semaphore(name))

        hmh = fixed("hmh", [P, KD, T], F32R)
        hml = fixed("hml", [P, KD, T], F32R)
        raw = [fixed(f"raw{s}", [P, SLAB]) for s in range(2)]
        wh = [fixed(f"wh{s}", [P, SLAB], F32R) for s in range(2)]
        wl = [fixed(f"wl{s}", [P, SLAB], F32R) for s in range(2)]
        rope = fixed("rope", [P, 2, NS])
        rel = fixed("rel", [P, RELW], F16)
        pos = fixed("pos", [P, 2, NS], F16)
        mask = fixed("mask", [P, 896], F16)
        zpos = fixed("zpos", [P, 2])
        ident = fixed("ident", [P, P])
        ones = fixed("ones", [P, P])
        par_all = fixed("par_all", [P, DEPTH + 1, NPAR])
        decay_all = fixed("decay_all", [P, DEPTH + 1, 2 * RH])
        par = fixed("par", [P, NPAR])
        lg = fixed("lg", [P, 2 * RH])
        lt = fixed("lt", [P, 6, 2 * RH])
        lgh = fixed("lgh", [P, 3])
        gainh = fixed("gainh", [P, 2])
        zh = fixed("zh", [P, 2])
        cv = fixed("cv", [P, KD, 2])
        cs = fixed("cs", [P, KD, 2])
        mod = fixed("mod", [P, 6 * KD, 2])
        am1 = fixed("am1", [P, KD, 2])
        am2 = fixed("am2", [P, KD, 2])
        gm1 = fixed("gm1", [P, KD, 2])
        gm2 = fixed("gm2", [P, KD, 2])
        epsc = fixed("epsc", [P, 1])
        sums = fixed("sums", [P, 10])
        rsum = fixed("rsum", [P, 10])
        nmax = fixed("nmax", [P, 10])
        Z = top[0]

        class Map:
            def __init__(self, start):
                self.p = Z + start

            def __call__(self, name, shape, dt=F32):
                n = int(np.prod(shape[1:])) * (2 if dt == F16 else 4)
                t = at(name, shape, self.p, dt)
                self.p += -(-n // 32) * 32
                assert self.p <= room, (name, self.p, room)
                return t

        B = KD * T * 4
        merged = at("merged", [P, KD, T], Z)
        mix = at("mix", [P, KD, T], Z)
        x = at("x", [P, KD, T], Z + B)
        yret = at("yret", [P, KD, T], Z + B)
        r0 = Map(0)
        qs = r0("qs", [P, T]); ks = r0("ks", [P, T])
        kz_at = r0.p - Z
        qsw = r0("qsw", [P, NS]); ksw = r0("ksw", [P, NS])
        sg = r0("sg", [P, 2, T]); st = r0("st", [P, 2, DV]); xf = r0("xf", [P, 2, NS])
        assert r0.p <= Z + B, r0.p - Z - B
        r1 = Map(2 * B)
        qh = r1("qh", [P, T], F32R); ql = r1("ql", [P, T], F32R)
        kh = r1("kh", [P, T], F32R); kl = r1("kl", [P, T], F32R)
        qdh = r1("qdh", [P, 2, NS], F32R); qdl = r1("qdl", [P, 2, NS], F32R)
        vh = r1("vh", [P, 5, DV], F32R); vl = r1("vl", [P, 5, DV], F32R)
        ph = r1("ph", [P, 4 * NS + P], F32R); pl = r1("pl", [P, 4 * NS + P], F32R)
        dst = r1("dst", [P, RELW])
        s0r = r1("s0r", [P, 2, DV]); s0h = r1("s0h", [P, 2, DV], F32R); s0l = r1("s0l", [P, 2, DV], F32R)
        y = r1("y", [P, 2, T])
        pst_at = r1.p
        pst = r1("pst", [P, 2, NS])
        r1.p = pst_at
        sq2 = r1("sq2", [P, 2, T])
        r2 = Map(kz_at)
        kz = r2("kz", [P, 2, P]); kzh = r2("kzh", [P, 2, P], F32R); kzl = r2("kzl", [P, 2, P], F32R)
        m0 = Map(2 * B)
        yrh = m0("yrh", [P, KD, T], F32R); yrl = m0("yrl", [P, KD, T], F32R)
        gate = m0("gate", [P, 2, T])
        n0 = Map(B)
        yna = n0("yna", [P, NPAIR, T])
        nva = n0.p
        nv = n0("nv", [P, 5, 8, 2, 64], F32R)
        nvh, nvl = nv[:, :, :, 0, :], nv[:, :, :, 1, :]
        nqh = n0("nqh", [P, T], F32R); nql = n0("nql", [P, T], F32R)
        nkh = n0("nkh", [P, T], F32R); nkl = n0("nkl", [P, T], F32R)
        ckr = n0("ckr", [P, P]); ckh = n0("ckh", [P, P], F32R); ckl = n0("ckl", [P, P], F32R)
        cvr_at = n0.p - Z
        nkst = Map(cvr_at)("nkst", [P, P])
        cvr = n0("cvr", [P, NS]); cv_ = n0("cv_", [P, 8, 2, 64], F32R)
        cvh, cvl = cv_[:, :, 0, :], cv_[:, :, 1, :]
        bias = n0("bias", [P, BIASW]); strip = n0("strip", [P, 2, 384])
        s = n0("s", [P, 2, NS])
        pth = n0("pth", [P, 2, NS], F32R); ptl = n0("ptl", [P, 2, NS], F32R)
        nvst = Map(n0.p - Z)("nvst", [P, NS])
        o = n0("o", [P, 5, P])
        ada = [n0(f"ada{i}", [P, KD, P]) for i in range(RING)]
        m1 = Map(B)
        m1.p = nva
        ynh = m1("ynh", [P, NPAIR, T], F32R); ynl = m1("ynl", [P, NPAIR, T], F32R)
        gate4 = m1("gate4", [P, 4, T]); mtmp = m1("mtmp", [P, T])
        m2 = Map(0); m2.p = m1.p
        mh = m2("mh", [P, KD, T], F32R); ml = m2("ml", [P, KD, T], F32R)
        f0 = Map(2 * B)
        hidh = f0("hidh", [P, 2, 2, T], F32R); hidl = f0("hidl", [P, 2, 2, T], F32R)
        scratch_b = [f0(f"{n}_b", [P, T]) for n in ("ssq", "rstd")] + [f0("sq_b", [P, 2, T])]
        draw = f0("draw", [P, 2, D])
        dwh = f0("dwh", [P, 2, D], F32R); dwl = f0("dwl", [P, 2, D], F32R)
        sig = f0("sig", [P, T]); hid = f0("hid", [P, T])
        f1 = Map(2 * B)
        scratch_a = [f1(f"{n}_a", [P, T]) for n in ("ssq", "rstd")] + [f1("sq_a", [P, 2, T])]
        assert f1.p <= m1.p

        unit = [ctx.enter_context(nc.psum_tensor(f"unit{i}", [P, 2, 512], F32)) for i in range(2)]
        sc = [ctx.enter_context(nc.psum_tensor(f"sc{i}", [P, 512], F32)) for i in range(2)]
        tp = [ctx.enter_context(nc.psum_tensor(f"tp{i}", [P, 512], F32)) for i in range(2)]

        def sems(names):
            return [sem(n) for n in names.split()]

        raw_in, w_hi, w_lo = ([sem(f"{n}{i}") for i in range(2)] for n in ("raw_in", "w_hi", "w_lo"))
        ada_in = [sem(f"ada_in{i}") for i in range(RING)]
        unit_ready = sem("unit_ready")
        carried = sem("carried")
        o_ready = sem("o_ready")
        unit_free = [sem(f"unit_free{i}") for i in range(2)]
        unit_hi, const_in, const_set, ada_used, cs_ready, mod_ready = sems("unit_hi const_in const_set ada_used cs_ready mod_ready")
        d_in, d_hi, d_lo = sems("d_in d_hi d_lo")
        sq_ready, sq_used, rstd_ready, xt_ready, hmh_ready, hm_ready = sems("sq_ready sq_used rstd_ready xt_ready hmh_ready hm_ready")
        osq_ready, ssq_added, xn_ready, x_saved, x_back = sems("osq_ready ssq_added xn_ready x_saved x_back")
        lg_e, lg_z, lgh_ready, dexp_ready, swap_ready, roped, qk_hi, qk_ready = sems("lg_e lg_z lgh_ready dexp_ready swap_ready roped qk_hi qk_ready")
        qd_full, qd_hi, qd_ready, s0_in, s0_hi, s0_ready = sems("qd_full qd_hi qd_ready s0_in s0_hi s0_ready")
        sc_ready, p_full, p_hi, p_ready, kt_ready, kz_hi, kz_ready = sems("sc_ready p_full p_hi p_ready kt_ready kz_hi kz_ready")
        st_psum, st_ready, st_saved, ysq_ready, yret_ready = sems("st_psum st_ready st_saved ysq_ready yret_ready")
        yr_hi, yr_ready, merged_ready, yn_hi, yn_ready, m_hi, m_ready = sems("yr_hi yr_ready merged_ready yn_hi yn_ready m_hi m_ready")
        ck_in, ck_hi, ck_ready, cv_in, cv_hi, cv_ready, strip_in, strip_used = sems("ck_in ck_hi ck_ready cv_in cv_hi cv_ready strip_in strip_used")
        nsc_ready, s_ready, e_ready, t_ready, pt_hi, pt_ready, pt_used = sems("nsc_ready s_ready e_ready t_ready pt_hi pt_ready pt_used")
        nkst_ready, nvst_ready, nk_saved, nv_saved, y_saved = sems("nkst_ready nvst_ready nk_saved nv_saved y_saved")
        hid_hi, hid_ready = sems("hid_hi hid_ready")

        block = ctx.enter_context(nc.Block())

        def f32(ap):
            return ap.bitcast(F32)

        def wait_constants(engine):
            engine.wait_ge(const_in, 16 * 6)
            for s_ in (st_saved, nk_saved, nv_saved):
                engine.wait_ge(s_, 16)

        def carry(engine):
            engine.sem_inc(carried, 1)

        def halves(ap):
            return ap.rearrange("p (a b) -> p a b", a=2)

        def flat(ap):
            return ap.rearrange("p a b -> p (a b)")

        def row(ap):
            if len(ap.shape) == 3:
                return ap.rearrange("a p n -> (a p) n")
            return ap.rearrange("a p b n -> (a p) b n")

        STREAMS = ((0, slice(0, NS)), (1, slice(NS, T)))

        @block.sync
        def _(sp):
            S = Slabs()
            rounds = Tally()

            def main(i, n):
                sp.wait_ge(w_lo[n], S.uses() + OPEN)
                sp.dma_start(raw[n][:, :], row(w_main[bass.ds(i, 1), :, :])).then_inc(raw_in[n], 16)
                S.add()

            def ada_round(first):
                for n in range(RING):
                    sp.wait_ge(ada_used, rounds.value() * RING + n + 1)
                    sp.dma_start(ada[n][:, :, :], w_ada[bass.ds(first + n, 1), :, :].rearrange("a p (k n) -> (a p) k n", k=KD))\
                      .then_inc(ada_in[n], 16)
                rounds.add()

            for n in range(2):
                main(n, n)
            with loop(sp, ADA_A // RING, {rounds: 1}) as i:
                ada_round(i * RING)
            with loop(sp, DEPTH, {S: MAIN, rounds: ADA // RING}) as l:
                with loop(sp, 6, {S: 2}) as i:
                    for n in range(2):
                        main(l * MAIN + i * 2 + n + 2, n)
                with loop(sp, KD // 2, {S: 2, rounds: 2}) as i:
                    for n in range(2):
                        main(l * MAIN + i * 2 + n + 14, n)
                        sp.wait_ge(yret_ready, (l + 1) * RH)
                        ada_round(l * ADA + i * 2 * RING + n * RING + ADA_A)
                with loop(sp, 3, {S: 2}) as i:
                    for n in range(2):
                        main(l * MAIN + i * 2 + n + 22, n)
                for n in range(6):
                    main(l * MAIN + n + 28, n % 2)
                    if n < ADA_A // RING:
                        ada_round(l * ADA + ADA + n * RING)
                with loop(sp, 13, {S: 2}) as i:
                    for n in range(2):
                        main(l * MAIN + i * 2 + n + 34, n)

        @block.gpsimd
        def _(g):
            for s_ in (*unit_free, *w_lo, s0_ready, ck_ready, strip_used, ssq_added, d_lo):
                g.sem_inc(s_, OPEN)
            g.sem_inc(ada_used, RING)
            g.memset(ones[:, :], 1.0).then_inc(const_set, 1)
            g.memset(epsc[:, :], EPS).then_inc(const_set, 1)
            g.dma_start(x[:, :, :], x_in).then_inc(x_back, 16)
            for to, of in ((par_all[:, :, :], params), (ident[:, :], ident_in), (rope[:, :, :], rope_in),
                           (rel[:, :], rel_in), (pos[:, :, :], pos_in), (mask[:, :], mask_in)):
                g.dma_start(to, of).then_inc(const_in, 16)
            g.dma_start(cv[:, :, :], cvec).then_inc(st_saved, 16)
            g.dma_start(decay_all[:, :, :], decay).then_inc(nk_saved, 16)
            g.dma_start(zpos[:, :], zpos_in).then_inc(nv_saved, 16)
            lay, heads, pairs, downs = (Tally() for _ in range(4))
            with loop(g, DEPTH, {lay: 1, heads: RH, pairs: NPAIR, downs: FB}) as l:
                g.wait_ge(hm_ready, lay.value() * 2 * KD + KD)
                carry(g)
                g.dma_start(x_keep, x[:, :, :]).then_inc(x_saved, 16)
                with loop(g, RH, {heads: 1}) as h:
                    g.wait_ge(s0_ready, heads.value() + OPEN)
                    carry(g)
                    g.dma_start(s0r[:, :, :], row(state_in[bass.ds(l * RH + h, 1), :, :, :])).then_inc(s0_in, 16)
                    g.wait_ge(st_ready, heads.value(1))
                    carry(g)
                    g.dma_start(row(state_out[bass.ds(l * RH + h, 1), :, :, :]), st[:, :, :]).then_inc(st_saved, 16)
                    heads.add()
                g.wait_ge(merged_ready, lay.value() * 2 * KD + KD)
                g.wait_ge(nk_saved, pairs.value() * 16 + 16)
                carry(g)
                g.dma_start(cvr[:, :], row(ctx_v[bass.ds(l, 1), :, :])).then_inc(cv_in, 16)
                g.wait_ge(nvst_ready, lay.value() * 2 + 2)
                carry(g)
                g.dma_start(row(v_out[bass.ds(l, 1), :, :]), nvst[:, :]).then_inc(nv_saved, 16)
                with loop(g, NPAIR, {pairs: 1}) as p:
                    g.wait_ge(ck_ready, pairs.value() + OPEN)
                    carry(g)
                    g.dma_start(ckr[:, :], row(ctx_k[bass.ds(l * NPAIR + p, 1), :, :])).then_inc(ck_in, 16)
                    g.wait_ge(strip_used, pairs.value() + OPEN)
                    carry(g)
                    g.dma_start(strip[:, :, :], row(strips[bass.ds(l * NPAIR + p, 1), :, :, :])).then_inc(strip_in, 16)
                    g.wait_ge(nkst_ready, pairs.value(1))
                    carry(g)
                    g.dma_start(row(k_out[bass.ds(l * NPAIR + p, 1), :, :]), nkst[:, :]).then_inc(nk_saved, 16)
                    pairs.add()
                g.wait_ge(merged_ready, lay.value() * 2 * KD + 2 * KD)
                g.wait_ge(x_saved, lay.value() * 16 + 16)
                carry(g)
                g.dma_start(x[:, :, :], x_keep).then_inc(x_back, 16)
                g.wait_ge(ssq_added, lay.value() * 2 * KD + KD + OPEN)
                carry(g)
                with loop(g, FB, {downs: 1}) as i:
                    g.wait_ge(d_lo, downs.value() + OPEN)
                    carry(g)
                    g.dma_start(draw[:, :, :],
                                w_down[bass.ds(l * FB + i, 1), :, :].rearrange("a p (k n) -> (a p) k n", k=2)).then_inc(d_in, 16)
                    downs.add()
                lay.add()
            g.wait_ge(xn_ready, 2 * DEPTH * KD)
            g.dma_start(x_out, x[:, :, :]).then_inc(y_saved, 16)
            g.wait_ge(st_saved, 16 * DEPTH * RH + 16)
            g.wait_ge(nk_saved, 16 * DEPTH * NPAIR + 16)
            g.wait_ge(nv_saved, 16 * DEPTH + 16)
            g.wait_ge(y_saved, 16)

        @block.tensor
        def _(pe):
            U = Units(pe, unit, unit_ready, unit_free)
            S = Slabs()
            lay, rounds, heads, pairs, sqs, downs = (Tally() for _ in range(6))

            def product(out, a, b, first, last):
                pe.matmul(out, a[0], b[0], start=first, stop=False)
                pe.matmul(out, a[0], b[1], start=False, stop=False)
                return pe.matmul(out, a[1], b[0], start=False, stop=last)

            def linear(w, acts, chunks, wait_chunk=None, between={}):
                u = U.take()
                for k in range(chunks):
                    if k in between:
                        between[k]()
                    if wait_chunk:
                        wait_chunk(k)
                    a, n, f, z = w(k), HALF, k == 0, k == chunks - 1
                    xs = [[t[:, k, h * n:(h + 1) * n] for t in acts] for h in range(2)]
                    for h in range(2):
                        pe.matmul(u[:, h, 0:n], a[0], xs[h][0], start=f, stop=False)
                        pe.matmul(u[:, h, 0:n], a[0], xs[h][1], start=False, stop=False)
                    for h in range(2):
                        mm = pe.matmul(u[:, h, 0:n], a[1], xs[h][0], start=False, stop=z)
                U.give(mm)

            def slab(cols, chunks, wait=True):
                s_ = S.slot()
                pe.wait_ge(w_lo[s_], S.uses() + 1 + OPEN)
                S.add()
                hi, lo = (t[s_][:, 0:chunks * cols].rearrange("p (k n) -> p k n", k=chunks) for t in (wh, wl))
                return lambda c: (lambda k: (hi[:, k, c * P:(c + 1) * P], lo[:, k, c * P:(c + 1) * P])), hi, lo

            def values():
                _, hi, lo = slab(256, KD)
                for tiles in (range(4), range(4, 5)):
                    u = U.take()
                    for t in tiles:
                        out = u[:, t % 4 // 2, t % 2 * 256:t % 2 * 256 + 256]
                        for k in range(KD):
                            a = [m[:, k, t * P:(t + 1) * P] for m in (hmh, hml)]
                            mm = product(out, a, (hi[:, k, :], lo[:, k, :]), k == 0, k == KD - 1)
                    U.give(mm)

            def stats(sq):
                u = U.take()
                for c in range(KD):
                    pe.wait_ge(sq_ready, sqs.value(c + 1))
                    for h in range(2):
                        mm = pe.matmul(u[:, h, 0:HALF], ones[:, :], sq[:, c % 2, h * HALF:(h + 1) * HALF],
                                       start=c == 0, stop=c == KD - 1)
                    if c < KD - 2:
                        mm.then_inc(sq_used, 1)
                U.give(mm)
                sqs.add(KD)

            def total(ssq, which):
                pe.wait_ge(ssq_added, which + OPEN)
                u = U.take()
                for h in range(2):
                    mm = pe.matmul(u[:, h, 0:HALF], ones[:, :], ssq[:, h * HALF:(h + 1) * HALF], start=True, stop=True)
                U.give(mm)

            pe.wait_ge(const_set, 2)
            wait_constants(pe)
            def ada_chunk(slot, chunk):
                pe.wait_ge(ada_in[slot], rounds.value(1) * 16)
                for k in range(KD):
                    mm = pe.matmul(tp[0][:, bass.ds(chunk * 2, 2)], ada[slot][:, k, :], cs[:, k, :], start=k == 0, stop=k == KD - 1)
                mm.then_inc(ada_used, 1)
                if slot == RING - 1:
                    rounds.add()

            stats(scratch_b[2])
            pe.wait_ge(cs_ready, 1)
            with loop(pe, ADA_A // RING, {rounds: 1}) as i:
                for n in range(RING):
                    ada_chunk(n, i * RING + n)
            per_layer = {U: 240, S: MAIN, lay: 1, rounds: ADA // RING, heads: RH, pairs: NPAIR, sqs: 2 * KD, downs: FB}
            with loop(pe, DEPTH, per_layer) as l:
                def hm_wait(part):
                    return lambda k: pe.wait_ge(hm_ready, lay.value() * 2 * KD + part * KD + k + 1)

                with loop(pe, RH // 2, {U: 20, S: 6, heads: 2}):
                    for hh in range(2):
                        w, _, _ = slab(256, KD)
                        linear(w(0), (hmh, hml), KD, hm_wait(0) if hh == 0 else None)
                        linear(w(1), (hmh, hml), KD)
                        values()
                        pe.wait_ge(qk_ready, heads.value() * 2 + 2)
                        pe.transpose(tp[0][:, 0:P], ks[:, NS:T], ident[:, :]).then_inc(kt_ready, 1)

                        def score(i):
                            if i >= 2:
                                pe.wait_ge(p_full, heads.value() * 5 + i - 1)
                            n = NS if i < 4 else P
                            keys = [t[:, i * P:(i + 1) * P] for t in (kh, kl)]
                            qrs = [t[:, 0:NS] if i < 4 else t[:, NS:T] for t in (qh, ql)]
                            product(sc[i % 2][:, 0:n], keys, qrs, True, True).then_inc(sc_ready, 1)

                        score(0)
                        score(1)
                        w, _, _ = slab(256, KD)
                        linear(w(0), (hmh, hml), KD)
                        score(2)
                        score(3)
                        linear(w(1), (hmh, hml), KD)
                        score(4)
                        pe.wait_ge(s0_ready, heads.value(1) + OPEN)
                        pe.wait_ge(qd_ready, heads.value(1))
                        for c in range(2):
                            u = U.take()
                            cols = slice(c * P, (c + 1) * P)
                            for i in range(4):
                                if c == 0:
                                    pe.wait_ge(p_ready, heads.value() * 5 + i + 1)
                                product(u[:, 0, :], (vh[:, i, cols], vl[:, i, cols]),
                                        (ph[:, i * NS:(i + 1) * NS], pl[:, i * NS:(i + 1) * NS]), i == 0, False)
                            for d in range(2):
                                product(u[:, 0, :], (s0h[:, d, cols], s0l[:, d, cols]),
                                        (qdh[:, d, :], qdl[:, d, :]), False, d == 1)
                            if c == 0:
                                pe.wait_ge(p_ready, heads.value() * 5 + 5)
                            U.give(product(u[:, 1, 0:P], (vh[:, 4, cols], vl[:, 4, cols]),
                                           (ph[:, 4 * NS:], pl[:, 4 * NS:]), True, True))
                        pe.wait_ge(kz_ready, heads.value(1))
                        for d in range(2):
                            mm = product(tp[1][:, d * DV:(d + 1) * DV], (kzh[:, d, :], kzl[:, d, :]),
                                         (vh[:, 4, :], vl[:, 4, :]), True, True)
                        mm.then_inc(st_psum, 1)
                        U.wait_released(1)
                        u = U.take()
                        for h in range(2):
                            for c in range(2):
                                mm = pe.matmul(u[:, h, 0:HALF], ones[:, :], y[:, c, h * HALF:(h + 1) * HALF],
                                               start=c == 0, stop=c == 1)
                        U.give(mm)
                        pe.wait_ge(ysq_ready, heads.value(1))
                        u = U.take()
                        for h in range(2):
                            for c in range(2):
                                mm = pe.matmul(u[:, h, 0:HALF], ones[:, :], sq2[:, c, h * HALF:(h + 1) * HALF],
                                               start=c == 0, stop=c == 1)
                        U.give(mm)
                        heads.add()
                with loop(pe, KD // 2, {U: 4, S: 2, rounds: 2}) as j:
                    def ada_next(n):
                        return lambda: ada_chunk(n % RING, j * 8 + n)
                    w, _, _ = slab(256, KD)
                    linear(w(0), (hmh, hml), KD)
                    linear(w(1), (hmh, hml), KD, None, {5: ada_next(0)})
                    ada_next(1)()
                    w, _, _ = slab(256, KD)
                    for n in range(2):
                        linear(w(n), (yrh, yrl), KD, (lambda k: pe.wait_ge(yr_ready, lay.value() * KD + k + 1)) if n == 0 else None,
                               {3: ada_next(2 + 3 * n), 6: ada_next(3 + 3 * n)})
                        ada_next(4 + 3 * n)()
                for _ in range(2):
                    values()
                pe.wait_ge(cv_ready, lay.value(1))
                carry(pe)
                with loop(pe, NPAIR // 2, {U: 10, S: 2, pairs: 2}) as pp:
                    for ph_ in range(2):
                        w, _, _ = slab(256, KD)
                        linear(w(0), (hmh, hml), KD)
                        linear(w(1), (hmh, hml), KD)
                        U.wait_released(2)
                        U.wait_released(1)
                        pe.wait_ge(ck_ready, pairs.value(1) + OPEN)
                        ou = None

                        def score(v):
                            hh, j = divmod(v, 5)
                            if v >= 2:
                                pe.wait_ge(s_ready, pairs.value() * 10 + v - 1)
                            rows = slice(64 * hh, 64 * hh + 64)
                            if j < 4:
                                first, tiles, _ = BLOCKS[j]
                                n = tiles * P
                                q = [t[rows, j * P:(j + 1) * P] for t in (nqh, nql)]
                                product(sc[v % 2][:, 0:n], q, [t[rows, first * P:first * P + n] for t in (nkh, nkl)], True, True)
                                mm = product(sc[v % 2][:, n:n + P], q, [t[rows, :] for t in (ckh, ckl)], True, True)
                            else:
                                mm = product(sc[v % 2][:, 0:P], [t[rows, NS:T] for t in (nqh, nql)],
                                             [t[rows, NS:T] for t in (nkh, nkl)], True, True)
                            mm.then_inc(nsc_ready, 1)

                        def turn(v):
                            n = BLOCKS[v % 5][1] + 1 if v % 5 < 4 else 1
                            pe.wait_ge(e_ready, pairs.value() * 10 + v + 1)
                            if v >= 2:
                                pe.wait_ge(pt_ready, pairs.value() * 10 + v - 1)
                            for i in range(n):
                                mm = pe.transpose(tp[v % 2][:, i * P:(i + 1) * P], s[:, v % 2, i * P:(i + 1) * P], ident[:, :])
                            mm.then_inc(t_ready, 1)

                        def weigh(v, u):
                            hh, j = divmod(v, 5)
                            pe.wait_ge(pt_ready, pairs.value() * 10 + v + 1)
                            out = u[:, 0, j * P:(j + 1) * P] if j < 4 else u[:, 1, 0:P]
                            tiles = [BLOCKS[j][0] + i for i in range(BLOCKS[j][1])] + ["ctx"] if j < 4 else [4]
                            head = pp * 4 + (ph_ * 2 + hh)
                            for i, t in enumerate(tiles):
                                vals = (cv_ if t == "ctx" else nv[:, t])[:, bass.ds(head, 1)].rearrange("p a b n -> p (a b n)")
                                pe.matmul(out, pth[:, v % 2, i * P:(i + 1) * P], vals, start=i == 0, stop=False)
                                mm = pe.matmul(out[:, 0:64], ptl[:, v % 2, i * P:(i + 1) * P], vals[:, 0:64],
                                               start=False, stop=i == len(tiles) - 1)
                            if v < 9:
                                mm.then_inc(pt_used, 1)
                            return mm

                        for v in range(13):
                            if v < 10:
                                score(v)
                            if v == 3:
                                ou = U.take()
                            if v == 8:
                                U.add()
                                ou = U.take()
                            if v >= 3:
                                mm = weigh(v - 3, ou)
                            if 1 <= v < 11:
                                turn(v - 1)
                        mm.then_inc(unit_ready, 2)
                        U.add()
                        U.wait_released(1)
                        U.wait_released(2)
                        pe.wait_ge(o_ready, pairs.value(1))
                        u = U.take()
                        for t in range(5):
                            mm = pe.transpose(u[:, t // 4, t % 4 * P:(t % 4 + 1) * P], o[:, t, :], ident[:, :])
                        U.give(mm)
                        pairs.add()
                for J in range(2):
                    for n in range(2):
                        w, _, _ = slab(256, KD)
                        for c in range(2):
                            linear(w(c), (hmh, hml), KD)
                            ada_chunk((2 * n + c) % RING, 8 * J + 2 * n + c)
                    w, _, _ = slab(512, NPAIR)
                    for c in range(4):
                        linear(w(c), (ynh, ynl), NPAIR,
                               (lambda k: pe.wait_ge(yn_ready, lay.value() * NPAIR + k + 1)) if J == 0 and c == 0 else None)
                        ada_chunk(c, 8 * J + 4 + c)
                with loop(pe, 2, {U: 4, S: 2}):
                    for n in range(2):
                        w, _, _ = slab(256, KD)
                        linear(w(0), (mh, ml), KD, (lambda k: pe.wait_ge(m_ready, lay.value() * KD + k + 1)) if n == 0 else None)
                        linear(w(1), (mh, ml), KD)
                total(scratch_a[0], lay.value() * 2 * KD + KD)
                stats(scratch_a[2])

                def gate_up(first=False):
                    for n in range(2):
                        w, _, _ = slab(256, KD)
                        linear(w(0), (hmh, hml), KD, hm_wait(1) if first and n == 0 else None)
                        linear(w(1), (hmh, hml), KD)

                def down(buf):
                    pe.wait_ge(d_lo, downs.value(1) + OPEN)
                    pe.wait_ge(hid_ready, downs.value(1) * 2)
                    for c in range(KD):
                        linear(lambda k: (dwh[:, k, c * P:(c + 1) * P], dwl[:, k, c * P:(c + 1) * P]),
                               (hidh[:, buf, :, :], hidl[:, buf, :, :]), 2)
                    downs.add()

                gate_up(first=True)
                with loop(pe, (FB - 1) // 2, {U: 24, S: 4, downs: 2}):
                    gate_up()
                    down(0)
                    gate_up()
                    down(1)
                down(0)
                total(scratch_b[0], lay.value() * 2 * KD + 2 * KD)
                stats(scratch_b[2])
                lay.add()

        @block.scalar
        def _(act):
            U = Units(act, unit, unit_ready, unit_free)
            S = Slabs()
            lay, heads, pairs, sqs, hms, downs, osq = (Tally() for _ in range(7))

            def split():
                U.wait_all_done()
                n = S.slot()
                act.wait_ge(raw_in[n], (S.uses() + 1) * 16)
                act.activation(wh[n][:, :], raw[n][:, :], ACT.Copy).then_inc(w_hi[n], 1)
                S.add()

            def hi_of_unit(out, view, scale=1.0):
                act.activation(out, view, ACT.Copy, scale=scale).then_inc(unit_hi, 1)

            def squares(sq):
                for c in range(KD):
                    if c >= 2:
                        act.wait_ge(sq_used, sqs.value() * 6 + c - 1)
                    yield c
                    act.activation(sq[:, c % 2, :], x[:, c, :], ACT.Square).then_inc(sq_ready, 1)
                sqs.add()

            def root(rstd):
                u = U.get()
                U.release(act.activation(halves(rstd[:, :]), u[:, :, 0:HALF], ACT.Sqrt, bias=epsc[:, 0:1], scale=1.0 / D))

            def modulated(t, shift_at):
                for c in range(KD):
                    act.wait_ge(xt_ready, hms.value(c + 1))
                    for i, cols in STREAMS:
                        a = act.activation(hmh[:, c, cols], t[:, c % 2, cols], ACT.Identity, bias=mod[:, shift_at + c, i:i + 1])
                    a.then_inc(hmh_ready, 1)
                hms.add(KD)

            act.wait_ge(const_set, 2)
            act.wait_ge(x_back, 16)
            for c in squares(scratch_b[2]):
                pass
            wait_constants(act)
            act.activation(cs[:, :, :], cv[:, :, :], ACT.Silu).then_inc(cs_ready, 1)
            act.wait_ge(lg_z, 1)
            act.activation(lt[:, 0, :], lt[:, 1, :], ACT.Exp, scale=-1.0).then_inc(lg_e, 1)
            for n in range(2):
                act.wait_ge(raw_in[n], 16)
                act.activation(wh[n][:, :], raw[n][:, :], ACT.Copy).then_inc(w_hi[n], 1)
                S.add()
            per_layer = {U: 240, S: MAIN, lay: 1, heads: RH, pairs: NPAIR, sqs: 2, hms: 2 * KD, downs: FB, osq: 2 * KD}
            with loop(act, DEPTH, per_layer) as l:
                root(scratch_b[1])
                act.wait_ge(mod_ready, lay.value() * 2 + 1)
                modulated(scratch_b[2], SH1)
                with loop(act, RH // 2, {U: 20, S: 6, heads: 2}):
                    for hh in range(2):
                        act.wait_ge(lgh_ready, heads.value(1))
                        act.activation(dst[:, :], dst[:, :], ACT.Exp)
                        for d in range(2):
                            act.activation(xf[:, d, :], pos[:, d, :], ACT.Exp, scale=lgh[:, d:d + 1])
                        for d in range(2):
                            a = act.activation(zh[:, d:d + 1], zpos[:, d:d + 1], ACT.Exp, scale=lgh[:, d:d + 1])
                        a.then_inc(dexp_ready, 1)
                        for to, scale in ((qs, 1.0), (ks, K_SCALE)):
                            u = U.get()
                            U.release(act.activation(halves(to[:, :]), u[:, :, 0:HALF], ACT.Copy, scale=scale))
                        act.drain()
                        for to, of in ((qsw, qs), (ksw, ks)):
                            act.activation(to[0:64, :], of[64:P, 0:NS], ACT.Copy)
                            act.activation(to[64:P, :], of[0:64, 0:NS], ACT.Copy).then_inc(swap_ready, 1)
                        split()
                        for n, (to, of) in enumerate(((qh, qs), (kh, ks))):
                            act.wait_ge(roped, heads.value() * 2 + n + 1)
                            act.activation(to[:, :], of[:, :], ACT.Copy).then_inc(qk_hi, 1)
                        act.wait_ge(qd_full, heads.value(1))
                        act.activation(qdh[:, 0, :], qsw[:, :], ACT.Copy)
                        act.activation(qdh[:, 1, :], ksw[:, :], ACT.Copy).then_inc(qd_hi, 1)
                        u = U.get()
                        hi_of_unit(vh[:, 0:4, :].rearrange("p (a b) n -> p a (b n)", a=2), u[:, :, :])
                        U.add()
                        u = U.get()
                        hi_of_unit(vh[:, 4, :], u[:, 0, 0:DV])
                        U.add()
                        split()
                        act.wait_ge(s0_in, heads.value(1) * 16)
                        act.activation(s0h[:, :, :], s0r[:, :, :], ACT.Copy).then_inc(s0_hi, 1)
                        act.wait_ge(kt_ready, heads.value(1))
                        act.wait_ge(qd_ready, heads.value(1))
                        for d in range(2):
                            act.activation(kz[:, d, :], tp[0][:, 0:P], ACT.Copy, scale=zh[:, d:d + 1])
                        act.drain()
                        act.activation(kzh[:, :, :], kz[:, :, :], ACT.Copy).then_inc(kz_hi, 1)

                        def p_split(i):
                            act.wait_ge(p_full, heads.value() * 5 + i + 1)
                            n = NS if i < 4 else P
                            act.activation(ph[:, i * NS:i * NS + n], pst[:, i % 2, 0:n], ACT.Copy).then_inc(p_hi, 1)

                        def gate_c(c):
                            u = U.get()
                            U.release(act.activation(halves(sg[:, c, :]), u[:, :, 0:HALF], ACT.Silu))

                        p_split(0)
                        p_split(1)
                        gate_c(0)
                        p_split(2)
                        p_split(3)
                        gate_c(1)
                        split()
                        p_split(4)
                        for c in range(2):
                            u = U.get()
                            act.activation(y[:, c, 0:NS], u[:, 0, :], ACT.Copy)
                            U.release(act.activation(y[:, c, NS:T], u[:, 1, 0:P], ACT.Copy))
                        act.wait_ge(st_psum, heads.value(1))
                        act.wait_ge(st_saved, heads.value() * 16 + 16)
                        act.activation(st[:, :, :], tp[1][:, :].rearrange("p (d n) -> p d n", d=2), ACT.Copy).then_inc(st_ready, 1)
                        U.add()
                        U.wait_released(1)
                        act.activation(sq2[:, :, :], y[:, :, :], ACT.Square).then_inc(ysq_ready, 1)
                        u = U.get()
                        U.release(act.activation(halves(qs[:, :]), u[:, :, 0:HALF], ACT.Sqrt, bias=epsc[:, 0:1], scale=1.0 / DV))
                        heads.add()
                act.wait_ge(yret_ready, heads.value())
                for c in range(KD):
                    act.activation(yrh[:, c, :], yret[:, c, :], ACT.Copy).then_inc(yr_hi, 1)
                with loop(act, KD // 2, {U: 4, S: 2}):
                    for c in range(2):
                        u = U.get()
                        U.release(act.activation(halves(gate[:, c, :]), u[:, :, 0:HALF], ACT.Sigmoid))
                    split()
                    U.add(2)
                    split()
                for n in range(2):
                    cols, hs = slice(n * 256, n * 256 + 256), slice(n * 4, n * 4 + 4)
                    u = U.get()
                    for a in range(2):
                        a_ = act.activation(nvh[:, 2 * a:2 * a + 2, hs, :], u[:, a, :].rearrange("p (t h n) -> p t h n", t=2, h=4), ACT.Copy)
                    a_.then_inc(unit_hi, 1)
                    U.add()
                    u = U.get()
                    if n == 0:
                        act.wait_ge(nv_saved, lay.value() * 16 + 16)
                    act.activation(nvst[:, cols], u[:, 0, 0:256], ACT.Copy).then_inc(nvst_ready, 1)
                    hi_of_unit(nvh[:, 4, hs, :], u[:, 0, 0:256].rearrange("p (h n) -> p h n", h=4))
                    U.add()
                    split()
                act.wait_ge(cv_in, lay.value(1) * 16)
                act.activation(cvh, cvr[:, :].rearrange("p (h n) -> p h n", h=8), ACT.Copy).then_inc(cv_hi, 1)
                with loop(act, NPAIR // 2, {U: 10, S: 2, pairs: 2}) as pp:
                    for ph_ in range(2):
                        for to, scale in ((nqh, -Q_SCALE), (nkh, 1.0)):
                            u = U.get()
                            if scale == 1.0:
                                act.wait_ge(cv_ready, lay.value(1))
                                act.wait_ge(nk_saved, pairs.value() * 16 + 16)
                                act.activation(nkst[:, :], u[:, 1, 192:HALF], ACT.Copy).then_inc(nkst_ready, 1)
                            hi_of_unit(halves(to[:, :]), u[:, :, 0:HALF], scale)
                            U.add()
                        split()
                        act.wait_ge(ck_in, pairs.value(1) * 16)
                        act.activation(ckh[:, :], ckr[:, :], ACT.Copy).then_inc(ck_hi, 1)

                        def width(v):
                            return (BLOCKS[v % 5][1] + 1) * P if v % 5 < 4 else P

                        for v in range(11):
                            if v < 10:
                                n = width(v)
                                act.wait_ge(s_ready, pairs.value() * 10 + v + 1)
                                act.activation(s[:, v % 2, 0:n], s[:, v % 2, 0:n], ACT.Exp, bias=nmax[:, v:v + 1], scale=-1.0,
                                               accum_out=sums[:, v:v + 1]).then_inc(e_ready, 1)
                            if v >= 1:
                                n = width(v - 1)
                                act.wait_ge(t_ready, pairs.value() * 10 + v)
                                if v >= 3:
                                    act.wait_ge(pt_used, pairs.value() * 9 + v - 2)
                                act.activation(pth[:, (v - 1) % 2, 0:n], tp[(v - 1) % 2][:, 0:n], ACT.Copy).then_inc(pt_hi, 1)
                        U.add(2)
                        u = U.get()
                        own = yna[:, bass.ds(pp * 2 + ph_, 1), :]
                        act.activation(flat(own)[:, NS:T], u[:, 1, 0:P], ACT.Copy)
                        U.release(act.activation(flat(own)[:, 0:NS], u[:, 0, :], ACT.Copy))
                        pairs.add()
                act.drain()
                for c in range(NPAIR):
                    act.activation(ynh[:, c, :], yna[:, c, :], ACT.Copy).then_inc(yn_hi, 1)
                for J in range(2):
                    for n in range(2):
                        for c in range(2):
                            u = U.get()
                            U.release(act.activation(halves(gate4[:, 2 * n + c, :]), u[:, :, 0:HALF], ACT.Sigmoid))
                        split()
                    U.add(4)
                    split()
                act.wait_ge(lg_z, lay.value() * 2 + 3)
                act.activation(lt[:, 0, :], lt[:, 1, :], ACT.Exp, scale=-1.0).then_inc(lg_e, 1)
                act.wait_ge(mod_ready, lay.value() * 2 + 2)
                act.wait_ge(nk_saved, pairs.value() * 16 + 16)
                for c in range(KD):
                    act.wait_ge(merged_ready, lay.value() * 2 * KD + KD + c + 1)
                    act.activation(mh[:, c, :], merged[:, c, :], ACT.Copy).then_inc(m_hi, 1)
                act.wait_ge(m_ready, lay.value() * KD + KD)
                with loop(act, 2, {U: 4, S: 2, osq: 4}) as i:
                    for n in range(4):
                        u = U.get()
                        if n >= 2:
                            act.wait_ge(ssq_added, osq.value(n - 1) + OPEN)
                        elif n == 0:
                            act.wait_ge(ssq_added, osq.value() + OPEN)
                        act.activation(halves(scratch_a[2][:, n % 2, :]), u[:, :, 0:HALF], ACT.Square).then_inc(osq_ready, 1)
                        U.release(act.activation(flat(mix[:, bass.ds(i * 4 + n, 1), :]).rearrange("p (a b) -> p a b", a=2),
                                                 u[:, :, 0:HALF], ACT.Copy))
                        if n % 2:
                            split()
                    osq.add(4)
                root(scratch_a[1])
                for c in squares(scratch_a[2]):
                    act.wait_ge(xn_ready, lay.value() * 2 * KD + c + 1)
                root(scratch_a[1])
                modulated(scratch_a[2], SH2)

                def gate_up(buf):
                    for n in range(2):
                        u = U.get()
                        U.release(act.activation(halves(sig[:, :]), u[:, :, 0:HALF], ACT.Silu))
                        U.add()
                        U.wait_released(1)
                        act.activation(hidh[:, buf, n, :], hid[:, :], ACT.Copy).then_inc(hid_hi, 1)
                        split()

                def down_split():
                    U.wait_all_done()
                    act.wait_ge(d_in, downs.value(1) * 16)
                    act.activation(dwh[:, :, :], draw[:, :, :], ACT.Copy).then_inc(d_hi, 1)
                    downs.add()

                gate_up(0)
                down_split()
                with loop(act, (FB - 1) // 2, {U: 24, S: 4, downs: 2}):
                    for buf in (1, 0):
                        gate_up(buf)
                        U.add(KD)
                        down_split()
                for c in range(KD):
                    U.add()
                    U.wait_released(1)
                    if c >= 2:
                        act.wait_ge(ssq_added, osq.value(c - 1) + OPEN)
                    act.activation(scratch_b[2][:, c % 2, :], mix[:, c, :], ACT.Square).then_inc(osq_ready, 1)
                osq.add(KD)
                root(scratch_b[1])
                for c in squares(scratch_b[2]):
                    act.wait_ge(xn_ready, lay.value() * 2 * KD + KD + c + 1)
                lay.add()

        @block.vector
        def _(dve):
            U = Units(dve, unit, unit_ready, unit_free)
            S = Slabs()
            lay, heads, pairs, hms, downs, hids, osq, his, consts, ada_done = (Tally() for _ in range(10))

            def split():
                n = S.slot()
                dve.wait_ge(w_hi[n], S.uses() + 1)
                dve.tensor_tensor(wl[n][:, :], raw[n][:, :], f32(wh[n][:, :]), ALU.subtract).then_inc(w_lo[n], 1)
                S.add()

            def lo(out, full, hi):
                return dve.tensor_tensor(out, full, f32(hi), ALU.subtract)

            def wait_hi():
                his.add()
                dve.wait_ge(unit_hi, his.value())

            def inverse_root(rstd):
                U.add()
                U.wait_released(1)
                dve.reciprocal(rstd[:, :], rstd[:, :])
                dve.drain()

            def modulate(t, rstd, scale, shift_at):
                for c in range(KD + 1):
                    if c < KD:
                        if c >= 2:
                            dve.drain()
                        for i, cols in STREAMS:
                            a = dve.scalar_tensor_tensor(out=t[:, c % 2, cols], in0=x[:, c, cols], scalar=scale[:, c, i:i + 1],
                                                         in1=rstd[:, cols], op0=ALU.mult, op1=ALU.mult)
                        a.then_inc(xt_ready, 1)
                    if c >= 1:
                        dve.wait_ge(hmh_ready, hms.value(c))
                        for i, cols in STREAMS:
                            a = dve.scalar_tensor_tensor(out=hml[:, c - 1, cols], in0=t[:, (c - 1) % 2, cols],
                                                         scalar=mod[:, shift_at + c - 1, i:i + 1], in1=f32(hmh[:, c - 1, cols]),
                                                         op0=ALU.add, op1=ALU.subtract)
                        a.then_inc(hm_ready, 1)
                hms.add(KD)

            def residual(rstd, gains):
                for c in range(0, KD, 2):
                    for n in range(2):
                        for i, cols in STREAMS:
                            dve.scalar_tensor_tensor(out=mix[:, c + n, cols], in0=mix[:, c + n, cols], scalar=gains[:, c + n, i:i + 1],
                                                     in1=rstd[:, cols], op0=ALU.mult, op1=ALU.mult)
                    dve.drain()
                    for n in range(2):
                        dve.tensor_tensor(x[:, c + n, :], x[:, c + n, :], mix[:, c + n, :], ALU.add).then_inc(xn_ready, 1)

            def sum_squares(sq, ssq, n, half=0):
                for c in range(n):
                    dve.drain()
                    dve.wait_ge(osq_ready, osq.value(c + 1))
                    dve.tensor_tensor(ssq[:, :], ssq[:, :], sq[:, (c + half) % 2, :], ALU.add).then_inc(ssq_added, 1)
                osq.add(n)

            def layer_constants(l):
                dve.tensor_copy(par[:, :], flat(par_all[:, bass.ds(l, 1), :]))
                dve.tensor_copy(lt[:, 5, :], flat(decay_all[:, bass.ds(l, 1), :]))
                dve.drain()
                dve.tensor_scalar(lt[:, 2, :], lt[:, 5, :], -1.0, None, ALU.mult)
                dve.drain()
                dve.tensor_tensor(lt[:, 1, :], lt[:, 5, :], lt[:, 2, :], ALU.max).then_inc(lg_z, 1)
                dve.wait_ge(lg_e, consts.value(1))
                dve.tensor_scalar(lt[:, 2, :], lt[:, 0, :], 2.0, None, ALU.add)
                dve.drain()
                dve.reciprocal(lt[:, 2, :], lt[:, 2, :])
                dve.drain()
                dve.tensor_tensor(lt[:, 2, :], lt[:, 0, :], lt[:, 2, :], ALU.mult)
                dve.drain()
                dve.tensor_tensor(lt[:, 3, :], lt[:, 2, :], lt[:, 2, :], ALU.mult)
                dve.drain()
                dve.tensor_scalar(lt[:, 4, :], lt[:, 3, :], 1.0 / 15, None, ALU.mult)
                for n in (13, 11, 9, 7, 5, 3):
                    dve.drain()
                    dve.scalar_tensor_tensor(out=lt[:, 4, :], in0=lt[:, 4, :], scalar=1.0 / n, in1=lt[:, 3, :], op0=ALU.add, op1=ALU.mult)
                dve.drain()
                dve.scalar_tensor_tensor(out=lt[:, 4, :], in0=lt[:, 4, :], scalar=1.0, in1=lt[:, 2, :], op0=ALU.add, op1=ALU.mult)
                dve.tensor_scalar(lt[:, 5, :], lt[:, 5, :], 0.0, None, ALU.min)
                dve.drain()
                dve.scalar_tensor_tensor(out=lg[:, :], in0=lt[:, 4, :], scalar=-2.0, in1=lt[:, 5, :], op0=ALU.mult, op1=ALU.add)\
                   .then_inc(lg_z, 1)
                consts.add()
                modulation(0, ADA_A, ADA_A, ((am1, SC1, N_PRE_MIX, 1.0),))

            def modulation(first, n, used, parts):
                ada_done.add(used)
                dve.wait_ge(ada_used, ada_done.value() + RING)
                dve.tensor_tensor(mod[:, first:first + n, :], tp[0][:, 0:2 * n].rearrange("p (c s) -> p c s", s=2),
                                  par[:, B_ADA + first:B_ADA + first + n].unsqueeze(2).broadcast_to([P, n, 2]), ALU.add)
                dve.drain()
                for out, part, gain, plus in parts:
                    a = dve.scalar_tensor_tensor(out=out[:, :, :], in0=mod[:, part:part + KD, :], scalar=plus,
                                                 in1=par[:, gain:gain + KD].unsqueeze(2).broadcast_to([P, KD, 2]),
                                                 op0=ALU.add, op1=ALU.mult)
                a.then_inc(mod_ready, 1)

            wait_constants(dve)
            layer_constants(0)
            split()
            split()
            per_layer = {U: 240, S: MAIN, lay: 1, heads: RH, pairs: NPAIR, hms: 2 * KD, downs: FB, hids: 2 * FB,
                         osq: 2 * KD, his: 2 * RH + 4 + 2 * NPAIR, consts: 1, ada_done: ADA}
            with loop(dve, DEPTH, per_layer) as l:
                inverse_root(scratch_b[1])
                modulate(scratch_b[2], scratch_b[1], am1, SH1)
                with loop(dve, RH // 2, {U: 20, S: 6, heads: 2, his: 4}) as hp:
                    for hh in range(2):
                        head = hp * 2 + hh
                        dve.drain()
                        dve.tensor_copy(lgh[:, 0:1], lg[:, bass.ds(head, 1)])
                        dve.tensor_copy(gainh[:, :], par[:, bass.ds(head * 2 + GN, 2)])
                        dve.tensor_copy(lgh[:, 1:2], lg[:, bass.ds(head + RH, 1)])
                        dve.drain()
                        dve.tensor_scalar(lgh[:, 2:3], lgh[:, 1:2], -1.0, None, ALU.mult)
                        dve.drain()
                        dve.tensor_scalar(dst[:, :], rel[:, :], lgh[:, 2:3], None, ALU.mult)
                        dve.drain()
                        dve.scalar_tensor_tensor(out=dst[:, :], in0=rel[:, :], scalar=lgh[:, 0:1], in1=dst[:, :],
                                                 op0=ALU.mult, op1=ALU.min).then_inc(lgh_ready, 1)
                        dve.wait_ge(dexp_ready, heads.value(1))
                        for at_ in (DIAG, CTX_DIAG):
                            dve.tensor_tensor(dst[:, at_:at_ + P], dst[:, at_:at_ + P], ident[:, :], ALU.add)
                        U.add(2)
                        for n, (a, b) in enumerate(((qs, qsw), (ks, ksw))):
                            dve.wait_ge(swap_ready, heads.value() * 2 + n + 1)
                            dve.tensor_tensor(a[:, 0:NS], a[:, 0:NS], rope[:, 0, :], ALU.mult)
                            dve.tensor_tensor(b[:, :], b[:, :], rope[:, 1, :], ALU.mult)
                            dve.drain()
                            dve.tensor_tensor(a[:, 0:NS], a[:, 0:NS], b[:, :], ALU.add).then_inc(roped, 1)
                        split()
                        for n, (to, of, hi) in enumerate(((ql, qs, qh), (kl, ks, kh))):
                            dve.wait_ge(qk_hi, heads.value() * 2 + n + 1)
                            lo(to[:, :], of[:, :], hi[:, :]).then_inc(qk_ready, 1)
                        dve.tensor_tensor(qsw[:, :], qs[:, 0:NS], xf[:, 0, :], ALU.mult)
                        dve.tensor_tensor(ksw[:, :], qs[:, 0:NS], xf[:, 1, :], ALU.mult).then_inc(qd_full, 1)
                        dve.wait_ge(qd_hi, heads.value(1))
                        lo(qdl[:, 0, :], qsw[:, :], qdh[:, 0, :])
                        lo(qdl[:, 1, :], ksw[:, :], qdh[:, 1, :]).then_inc(qd_ready, 1)
                        wait_hi()
                        u = U.get()
                        U.release(lo(vl[:, 0:4, :].rearrange("p (a b) n -> p a (b n)", a=2), u[:, :, :],
                                     vh[:, 0:4, :].rearrange("p (a b) n -> p a (b n)", a=2)))
                        wait_hi()
                        u = U.get()
                        U.release(lo(vl[:, 4, :], u[:, 0, 0:DV], vh[:, 4, :]))
                        split()
                        dve.wait_ge(s0_hi, heads.value(1))
                        lo(s0l[:, :, :], s0r[:, :, :], s0h[:, :, :]).then_inc(s0_ready, 1)

                        def decay_(i):
                            dve.wait_ge(sc_ready, heads.value() * 5 + i + 1)
                            n, at_ = (NS, DIAG - P * i) if i < 4 else (P, CTX_DIAG)
                            dve.tensor_tensor(pst[:, i % 2, 0:n], sc[i % 2][:, 0:n], dst[:, at_:at_ + n], ALU.mult)\
                               .then_inc(p_full, 1)

                        def p_lo(i):
                            n = NS if i < 4 else P
                            dve.wait_ge(p_hi, heads.value() * 5 + i + 1)
                            lo(pl[:, i * NS:i * NS + n], pst[:, i % 2, 0:n], ph[:, i * NS:i * NS + n]).then_inc(p_ready, 1)

                        decay_(0)
                        decay_(1)
                        dve.wait_ge(kz_hi, heads.value(1))
                        lo(kzl[:, :, :], kz[:, :, :], kzh[:, :, :]).then_inc(kz_ready, 1)
                        p_lo(0)
                        p_lo(1)
                        dve.drain()
                        decay_(2)
                        decay_(3)
                        p_lo(2)
                        p_lo(3)
                        split()
                        dve.drain()
                        decay_(4)
                        p_lo(4)
                        U.add(4)
                        u = U.get()
                        for c in range(2):
                            a = dve.scalar_tensor_tensor(out=halves(y[:, c, :]), in0=u[:, :, 0:HALF], scalar=-1.0 / DV,
                                                         in1=halves(y[:, c, :]), op0=ALU.mult, op1=ALU.add)
                        U.release(a)
                        inverse_root(qs)
                        dve.tensor_tensor(y[:, :, :], y[:, :, :], qs[:, :].unsqueeze(1).broadcast_to([P, 2, T]), ALU.mult)
                        dve.drain()
                        if hh == 0:
                            dve.wait_ge(x_saved, lay.value(1) * 16)
                        for c in range(2):
                            a = dve.scalar_tensor_tensor(out=flat(yret[:, bass.ds(head * 2 + c, 1), :]), in0=y[:, c, :],
                                                         scalar=gainh[:, c:c + 1], in1=sg[:, c, :], op0=ALU.mult, op1=ALU.mult)
                        a.then_inc(yret_ready, 1)
                        heads.add()
                dve.drain()
                dve.wait_ge(st_saved, heads.value() * 16 + 16)
                for c in range(KD):
                    dve.wait_ge(yr_hi, lay.value() * KD + c + 1)
                    lo(yrl[:, c, :], yret[:, c, :], yrh[:, c, :]).then_inc(yr_ready, 1)
                with loop(dve, KD // 2, {U: 4, S: 2}) as j:
                    U.add(2)
                    split()
                    for c in range(2):
                        u = U.get()
                        U.wait_released(2)
                        a = dve.tensor_tensor(flat(merged[:, bass.ds(j * 2 + c, 1), :]).rearrange("p (a b) -> p a b", a=2),
                                              u[:, :, 0:HALF], halves(gate[:, c, :]), ALU.mult)
                        U.release(a)
                    split()
                modulation(ADA_A, ADA_B, ADA_B, ((gm1, G1, N_POST_MIX, 0.0), (am2, SC2, N_PRE_FFN, 1.0),
                                                 (gm2, G2, N_POST_FFN, 0.0)))
                dve.drain()
                for k_, at_ in enumerate(KIND_AT):
                    a = dve.memset(bias[:, at_ + KIND_W[k_]:at_ + KIND_W[k_] + P], 0.0)
                a.then_inc(merged_ready, KD)
                for n in range(2):
                    cols, hs = slice(n * 256, n * 256 + 256), slice(n * 4, n * 4 + 4)
                    wait_hi()
                    u = U.get()
                    for a in range(2):
                        a_ = lo(nvl[:, 2 * a:2 * a + 2, hs, :], u[:, a, :].rearrange("p (t h n) -> p t h n", t=2, h=4),
                                nvh[:, 2 * a:2 * a + 2, hs, :])
                    U.release(a_)
                    wait_hi()
                    u = U.get()
                    U.release(lo(nvl[:, 4, hs, :], u[:, 0, 0:256].rearrange("p (h n) -> p h n", h=4), nvh[:, 4, hs, :]))
                    split()
                dve.wait_ge(cv_hi, lay.value(1))
                lo(cvl, cvr[:, :].rearrange("p (h n) -> p h n", h=8), cvh).then_inc(cv_ready, 1)
                with loop(dve, NPAIR // 2, {U: 10, S: 2, pairs: 2, his: 4}):
                    for _ in range(2):
                        for to, hi, scale in ((nql, nqh, -Q_SCALE), (nkl, nkh, 1.0)):
                            u = U.get()
                            wait_hi()
                            U.release(dve.scalar_tensor_tensor(out=halves(to[:, :]), in0=u[:, :, 0:HALF], scalar=scale,
                                                               in1=f32(halves(hi[:, :])), op0=ALU.mult, op1=ALU.subtract))
                        split()
                        dve.wait_ge(ck_hi, pairs.value(1))
                        lo(ckl[:, :], ckr[:, :], ckh[:, :]).then_inc(ck_ready, 1)
                        for v in range(11):
                            if v in (0, 5):
                                dve.drain()
                                if v == 0:
                                    dve.wait_ge(strip_in, pairs.value(1) * 16)
                                for kind in range(3):
                                    n = KIND_W[kind]
                                    a = dve.scalar_tensor_tensor(
                                        out=bias[:, KIND_AT[kind]:KIND_AT[kind] + n], in0=mask[:, MASK_AT[kind]:MASK_AT[kind] + n],
                                        scalar=BIG, in1=strip[:, v // 5, STRIP_AT[kind]:STRIP_AT[kind] + n],
                                        op0=ALU.mult, op1=ALU.subtract)
                                if v == 5:
                                    a.then_inc(strip_used, 1)
                                dve.drain()
                            if v < 10:
                                j = v % 5
                                if j < 4:
                                    at_, n = KIND_AT[BLOCKS[j][2]], KIND_W[BLOCKS[j][2]] + P
                                else:
                                    at_, n = KIND_W[0], P
                                dve.wait_ge(nsc_ready, pairs.value() * 10 + v + 1)
                                if v >= 2:
                                    dve.wait_ge(t_ready, pairs.value() * 10 + v - 1)
                                carry(dve)
                                dve.tensor_tensor_reduce(s[:, v % 2, 0:n], sc[v % 2][:, 0:n], bias[:, at_:at_ + n], 1.0, 3e38,
                                                         ALU.add, ALU.min, nmax[:, v:v + 1]).then_inc(s_ready, 1)
                            if v >= 1:
                                j = (v - 1) % 5
                                n = KIND_W[BLOCKS[j][2]] + P if j < 4 else P
                                dve.wait_ge(pt_hi, pairs.value() * 10 + v)
                                lo(ptl[:, (v - 1) % 2, 0:n], tp[(v - 1) % 2][:, 0:n], pth[:, (v - 1) % 2, 0:n]).then_inc(pt_ready, 1)
                        dve.reciprocal(rsum[:, :], sums[:, :])
                        dve.drain()
                        dve.wait_ge(nv_saved, lay.value(1) * 16 + 16)
                        for h in range(2):
                            u = U.get()
                            oh = o[:, :, h * 64:h * 64 + 64]
                            part = u[:, 0, :].rearrange("p (j b n) -> p j b n", j=4, b=2)
                            dve.tensor_copy(oh[:, 0:4, :], part[:, :, 1, :])
                            dve.tensor_copy(oh[:, 4, :], u[:, 1, 64:P])
                            dve.drain()
                            dve.tensor_tensor(oh[:, 0:4, :], oh[:, 0:4, :], part[:, :, 0, :], ALU.add)
                            U.release(dve.tensor_tensor(oh[:, 4, :], oh[:, 4, :], u[:, 1, 0:64], ALU.add))
                        dve.drain()
                        for h in range(2):
                            oh = o[:, :, h * 64:h * 64 + 64]
                            a = dve.tensor_tensor(oh, oh, rsum[:, 5 * h:5 * h + 5].unsqueeze(2).broadcast_to([P, 5, 64]), ALU.mult)
                        a.then_inc(o_ready, 1)
                        U.add()
                        pairs.add()
                dve.wait_ge(nk_saved, pairs.value() * 16 + 16)
                for c in range(NPAIR):
                    dve.wait_ge(yn_hi, lay.value() * NPAIR + c + 1)
                    lo(ynl[:, c, :], yna[:, c, :], ynh[:, c, :]).then_inc(yn_ready, 1)
                for J in range(2):
                    for n in range(2):
                        U.add(2)
                        split()
                    for c in range(4):
                        dve.drain()
                        u = U.get()
                        U.wait_released(4)
                        U.release(dve.tensor_tensor(halves(mtmp[:, :]), u[:, :, 0:HALF], halves(gate4[:, c, :]), ALU.mult))
                        dve.drain()
                        dve.tensor_tensor(merged[:, J * 4 + c, :], merged[:, J * 4 + c, :], mtmp[:, :], ALU.add)\
                           .then_inc(merged_ready, 1)
                    split()
                dve.drain()
                layer_constants(l + 1)
                for c in range(KD):
                    dve.wait_ge(m_hi, lay.value() * KD + c + 1)
                    lo(ml[:, c, :], merged[:, c, :], mh[:, c, :]).then_inc(m_ready, 1)
                dve.memset(scratch_a[0][:, :], 0.0)
                with loop(dve, 2, {U: 4, S: 2, osq: 4}):
                    for n in range(2):
                        U.add(2)
                        sum_squares(scratch_a[2], scratch_a[0], 2)
                        split()
                inverse_root(scratch_a[1])
                dve.wait_ge(x_back, (lay.value() + 2) * 16)
                residual(scratch_a[1], gm1)
                inverse_root(scratch_a[1])
                modulate(scratch_a[2], scratch_a[1], am2, SH2)

                def gate_up(buf, defer=False):
                    for n in range(2):
                        U.add()
                        dve.drain()
                        u = U.get()
                        U.wait_released(1)
                        U.release(dve.tensor_tensor(halves(hid[:, :]), u[:, :, 0:HALF], halves(sig[:, :]), ALU.mult))
                        hids.add()
                        dve.wait_ge(hid_hi, hids.value())
                        lo(hidl[:, buf, n, :], hid[:, :], hidh[:, buf, n, :]).then_inc(hid_ready, 1)
                        if n == 0 or not defer:
                            split()

                def down_split():
                    downs.add()
                    dve.wait_ge(d_hi, downs.value())
                    lo(dwl[:, :, :], draw[:, :, :], dwh[:, :, :]).then_inc(d_lo, 1)

                def down(chunks=range(KD)):
                    dve.drain()
                    for c in chunks:
                        u = U.get()
                        U.release(dve.tensor_tensor(halves(mix[:, c, :]), u[:, :, 0:HALF], halves(mix[:, c, :]), ALU.add))

                gate_up(0)
                for c in range(KD):
                    a = dve.memset(mix[:, c, :], 0.0)
                dve.memset(scratch_b[0][:, :], 0.0)
                down_split()
                with loop(dve, (FB - 1) // 2, {U: 24, S: 4, downs: 2, hids: 4}):
                    for buf in (1, 0):
                        gate_up(buf, defer=True)
                        down()
                        down_split()
                        split()
                for c in range(KD + 1):
                    if c < KD:
                        down(range(c, c + 1))
                    if c >= 1:
                        sum_squares(scratch_b[2], scratch_b[0], 1, (c - 1) % 2)
                inverse_root(scratch_b[1])
                residual(scratch_b[1], gm2)
                lay.add()


def slabs_of(w, cols):
    K, N = w.shape
    return w.reshape(K // P, P, N // cols, cols).transpose(2, 1, 0, 3).reshape(N // cols, P, K // P * cols)


def feature_major(v):
    return np.swapaxes(v.reshape(*v.shape[:-1], KD, P), -1, -2)


def main_slabs(w_in, w_gate, w_ret_out, w_na_out, w_o, w_fg, w_fu):
    q, k, v, g, nq, nk, nv = np.split(w_in, np.cumsum([512, 512, 1024, 1024, 512, 512]), axis=1)
    parts = []
    for h in range(RH):
        a, b = slice(h * P, (h + 1) * P), slice(h * DV, (h + 1) * DV)
        parts += [slabs_of(np.concatenate([q[:, a], k[:, a]], 1), 256), slabs_of(v[:, b], 256), slabs_of(g[:, b], 256)]
    for j in range(4):
        c = slice(j * 256, (j + 1) * 256)
        parts += [slabs_of(w_gate[:, :D][:, c], 256), slabs_of(w_ret_out[:, c], 256)]
    parts.append(slabs_of(nv, 256))
    for p in range(NPAIR):
        c = slice(p * P, (p + 1) * P)
        parts.append(slabs_of(np.concatenate([nq[:, c], nk[:, c]], 1), 256))
    for J in range(2):
        c = slice(J * 512, (J + 1) * 512)
        parts += [slabs_of(w_gate[:, D:][:, c], 256), slabs_of(w_na_out[:, c], 512)]
    parts.append(slabs_of(w_o, 256))
    for i in range(DFF // P):
        c = slice(i * P, (i + 1) * P)
        parts.append(slabs_of(np.concatenate([w_fg[:, c], w_fu[:, c]], 1), 256))
    return np.concatenate(parts, 0)


def window_strips(rpb):
    c, r, u, rk = np.ogrid[0:16, 0:GR, 0:48, 0:GR]
    dc, dr = np.broadcast_arrays(u - 16 - c + 15, rk - r + 7)
    ok = (dc >= 0) & (dc < 31)
    padded = np.pad(rpb, ((0, 0), (0, 0), (0, 0), (0, 1)))
    return padded[:, :, dr, np.where(ok, dc, 31)].reshape(rpb.shape[0] * NPAIR, 2, P, 384).transpose(0, 2, 1, 3)


def constants():
    t = np.arange(NS)
    t = t % GR * GW + t // GR
    inv = 10000.0 ** (-np.arange(32, dtype=np.float32) / 32)
    ang = np.concatenate([(t // GW).astype(np.float32)[:, None] * inv, (t % GW).astype(np.float32)[:, None] * inv], 1).T
    cos, sin = np.cos(ang), np.sin(ang)
    rope = np.stack([np.concatenate([cos, cos]), np.concatenate([-sin, sin])], 1).astype(np.float32)
    p, i, j = np.arange(P)[:, None], np.arange(P)[None, :], np.arange(CTX_DIAG)[None, :]
    rel = np.concatenate([(j % GR - p % GR) * GW + (j // GR - DIAG // GR) - p // GR, i - p], 1).astype(np.float16)
    pos = np.broadcast_to(np.stack([t + 1, NS - t])[None], (P, 2, NS)).astype(np.float16)
    zpos = np.concatenate([P - 1 - p, p], 1).astype(np.float32)
    masks = []
    for b, u0 in ((0, 16), (1, 0), (3, 0)):
        c = 16 * b + np.arange(16)[:, None, None, None]
        n = 384 if b == 1 else 256
        key = 16 * b - 16 + u0 + np.arange(n // GR)[None, None, :, None]
        start = np.clip(c - WIN // 2, 0, GW - WIN)
        m = np.where((key >= start) & (key < start + WIN), 0, 1)
        masks.append(np.broadcast_to(m, (16, GR, n // GR, GR)).reshape(P, n))
    mask = np.concatenate(masks, 1).astype(np.float16)
    return dict(rope=rope, rel=rel, pos=pos, mask=mask, zpos=zpos, ident=np.eye(P, dtype=np.float32))


def kernel(**inputs):
    import concourse.bacc as bacc
    from concourse.bass_utils import run_bass_kernel_spmd

    v = {k: np.asarray(a) for k, a in inputs.items()}
    arrays = {}
    by_column = v["x_sample"][0].reshape(GR, GW, D).transpose(1, 0, 2).reshape(NS, D)
    arrays["x"] = np.concatenate([by_column, v["x_prompt"][0]], 0).T.reshape(KD, P, T).transpose(1, 0, 2)
    mains = [main_slabs(*(v[n][l] for n in ("w_in", "w_gate", "w_ret_out", "w_na_out", "w_o", "w_ffn_gate", "w_ffn_up")))
             for l in range(DEPTH)]
    arrays["w_main"] = np.concatenate(mains + [mains[0][:2]], 0)
    arrays["w_down"] = v["w_ffn_down"].reshape(DEPTH * FB, 2, P, D).transpose(0, 2, 1, 3).reshape(DEPTH * FB, P, 2 * D)
    adas = [slabs_of(v["w_ada"][l], P) for l in range(DEPTH)]
    arrays["w_ada"] = np.concatenate(adas + [adas[0][:ADA_A]], 0)
    params = np.concatenate(
        [feature_major(v[n]) for n in ("norm_pre_mix", "norm_post_mix", "norm_pre_ffn", "norm_post_ffn", "ret_gn_gain")]
        + [v["b_ada"].reshape(DEPTH, 6 * KD, P).transpose(0, 2, 1)], -1).transpose(1, 0, 2)
    arrays["params"] = np.concatenate([params, params[:, :1]], 1)
    decay = v["ret_decay_logit"].reshape(1, DEPTH, 2 * RH)
    arrays["decay"] = np.broadcast_to(np.concatenate([decay, decay[:, :1]], 1), (P, DEPTH + 1, 2 * RH))
    arrays["state"] = v["state_ret"][0].transpose(0, 2, 3, 1, 4).reshape(DEPTH * RH, P, 2, DV)
    arrays["ctx_k"] = v["cache_na_k"][0].transpose(0, 2, 3, 1).reshape(DEPTH * NPAIR, P, P)
    arrays["ctx_v"] = v["cache_na_v"][0].reshape(DEPTH, P, NS)
    arrays["strips"] = window_strips(v["na_rpb"])
    arrays["cvec"] = np.stack([feature_major(v["c"][0]), feature_major(v["c_ctx"])], -1)
    arrays.update(constants())
    outs = {"x_out": (P, KD, T), "k_out": (DEPTH * NPAIR, P, P), "v_out": (DEPTH, P, NS), "state_out": (DEPTH * RH, P, 2, DV)}

    nc = bacc.Bacc("TRN2", target_bir_lowering=False, num_devices=1)
    args = []
    for name in list(arrays):
        arrays[name] = np.ascontiguousarray(arrays[name])
        args.append(nc.dram_tensor(name, arrays[name].shape, mybir.dt.from_np(arrays[name].dtype), kind="ExternalInput").ap())
    args += [nc.dram_tensor(name, shape, F32, kind="ExternalOutput").ap() for name, shape in outs.items()]
    args.append(nc.dram_tensor("x_keep", (P, KD, T), F32, kind="Internal").ap())
    build(nc, *args)
    r = run_bass_kernel_spmd(nc, [arrays], core_ids=[0]).results[0]
    x = r["x_out"].transpose(2, 1, 0).reshape(T, D)
    k = r["k_out"].reshape(1, DEPTH, NPAIR * 2, 64, P).transpose(0, 1, 4, 2, 3)
    vv = r["v_out"].reshape(1, DEPTH, P, NPAIR * 2, 64)
    st = r["state_out"].reshape(1, DEPTH, RH, P, 2, DV).transpose(0, 1, 4, 2, 3, 5)
    latent = x[:NS].reshape(GW, GR, D).transpose(1, 0, 2).reshape(1, NS, D)
    return (x[None, NS:], latent, k, vv, st)
```
